# Optimizing a Trainium2 kernel written in Bass

```python
import math
import jax, jax.numpy as jnp
from jax import lax
import numpy as np

D_MODEL = 1024
BATCH = 1
SEQ = 512
DEPTH = 1

HEAD_DIM = 64
FOX_HEADS = 8
SWA_HEADS = 8
SWA_KV_HEADS = 2
SWA_GROUP = SWA_HEADS // SWA_KV_HEADS
MIX_WIDTH = (FOX_HEADS + SWA_HEADS) * HEAD_DIM
WINDOW = 128
BLOCK = 128
N_BUCKETS = 32
MAX_DISTANCE = 128
N_EXPERTS = 32
TOP_K = 4
D_EXPERT = D_MODEL
SWIGLU_LIMIT = 7.0
SWIGLU_ALPHA = 1.702
EXPERT_BLOCK = 128
EPS = 1e-6
IN_SPLITS = (FOX_HEADS * HEAD_DIM, FOX_HEADS * HEAD_DIM, FOX_HEADS * HEAD_DIM, FOX_HEADS,
             SWA_HEADS * HEAD_DIM, SWA_KV_HEADS * HEAD_DIM, SWA_KV_HEADS * HEAD_DIM)
IN_WIDTH = sum(IN_SPLITS)

kernel_name = "hymba_fox_swa_sink_moe_layer"

def rms_norm(x, g):
    xf = x.astype(jnp.float32)
    y = xf * lax.rsqrt(jnp.mean(xf * xf, axis=-1, keepdims=True) + EPS)
    return (y * g.astype(jnp.float32)).astype(x.dtype)

def t5_bucket(n):
    max_exact = N_BUCKETS // 2
    nf = jnp.maximum(n, 1).astype(jnp.float32)
    large = max_exact + (jnp.log(nf / max_exact) / math.log(MAX_DISTANCE / max_exact)
                         * (N_BUCKETS - max_exact)).astype(jnp.int32)
    large = jnp.minimum(large, N_BUCKETS - 1)
    return jnp.where(n < max_exact, n, large)

def fox_attention(q, k, v, f_logit):
    b, s, h, dh = q.shape
    nb = s // BLOCK
    c = jnp.cumsum(jax.nn.log_sigmoid(f_logit.astype(jnp.float32)), axis=1).transpose(0, 2, 1)
    scale = dh ** -0.5
    kpos = jnp.arange(s)
    q_blocks = q.reshape(b, nb, BLOCK, h, dh).transpose(1, 0, 3, 2, 4)
    c_blocks = c.reshape(b, h, nb, BLOCK).transpose(2, 0, 1, 3)
    starts = jnp.arange(nb) * BLOCK

    def one_block(args):
        qb, cb, start = args
        logits = jnp.einsum('bhqd,bshd->bhqs', qb, k).astype(jnp.float32) * scale
        logits = logits + cb[..., None] - c[:, :, None, :]
        qpos = start + jnp.arange(BLOCK)
        causal = kpos[None, :] <= qpos[:, None]
        logits = jnp.where(causal, logits, -jnp.inf)
        p = jax.nn.softmax(logits, axis=-1).astype(v.dtype)
        return jnp.einsum('bhqs,bshd->bqhd', p, v)

    out = lax.map(one_block, (q_blocks, c_blocks, starts))
    return out.transpose(1, 0, 2, 3, 4).reshape(b, s, h * dh)

def swa_sink_attention(q, k, v, sinks, rel_bias):
    b, s, hq, dh = q.shape
    nb = s // BLOCK
    qb = q.reshape(b, nb, BLOCK, SWA_KV_HEADS, SWA_GROUP, dh)

    def band(t):
        tb = t.reshape(b, nb, BLOCK, SWA_KV_HEADS, dh)
        prev = jnp.pad(tb[:, :-1], ((0, 0), (1, 0), (0, 0), (0, 0), (0, 0)))
        return jnp.concatenate([prev, tb], axis=2)

    kw, vw = band(k), band(v)
    logits = jnp.einsum('bnqhgd,bnshd->bnhgqs', qb, kw).astype(jnp.float32) * dh ** -0.5
    qi = jnp.arange(BLOCK)[:, None]
    kj = jnp.arange(2 * BLOCK)[None, :]
    dist = qi + BLOCK - kj
    bias = rel_bias.astype(jnp.float32)[t5_bucket(jnp.maximum(dist, 0))]
    bias = bias.transpose(2, 0, 1).reshape(SWA_KV_HEADS, SWA_GROUP, BLOCK, 2 * BLOCK)
    key_pos = jnp.arange(nb)[:, None, None] * BLOCK - BLOCK + kj[None]
    valid = (dist >= 0) & (dist < WINDOW) & (key_pos >= 0)
    logits = jnp.where(valid[None, :, None, None], logits + bias, -jnp.inf)
    sink = jnp.broadcast_to(sinks.astype(jnp.float32).reshape(SWA_KV_HEADS, SWA_GROUP, 1, 1),
                            logits.shape[:-1] + (1,))
    probs = jax.nn.softmax(jnp.concatenate([logits, sink], axis=-1), axis=-1)[..., :-1].astype(v.dtype)
    out = jnp.einsum('bnhgqs,bnshd->bnqhgd', probs, vw)
    return out.reshape(b, s, hq * dh)

def moe_ffn(x, w_router, b_router, w_up_gate, b_up_gate, w_down, b_down):
    b, s, d = x.shape
    n = b * s
    xt = x.reshape(n, d)
    logits = (xt @ w_router).astype(jnp.float32) + b_router.astype(jnp.float32)
    top_val, top_idx = lax.top_k(logits, TOP_K)
    gates = jax.nn.softmax(top_val, axis=-1)
    n_assign = n * TOP_K
    e_flat = top_idx.reshape(-1).astype(jnp.int32)
    tok_flat = jnp.arange(n_assign, dtype=jnp.int32) // TOP_K
    g_flat = gates.reshape(-1)
    order = jnp.argsort(e_flat)
    e_sorted = e_flat[order]
    counts = jnp.zeros((N_EXPERTS,), jnp.int32).at[e_flat].add(1)
    padded = (counts + EXPERT_BLOCK - 1) // EXPERT_BLOCK * EXPERT_BLOCK
    start = jnp.cumsum(counts) - counts
    pstart = jnp.cumsum(padded) - padded
    pend = pstart + padded
    dest = pstart[e_sorted] + jnp.arange(n_assign, dtype=jnp.int32) - start[e_sorted]
    rows = n_assign + N_EXPERTS * EXPERT_BLOCK
    row_tok = jnp.full((rows,), n, jnp.int32).at[dest].set(tok_flat[order])
    row_gate = jnp.zeros((rows,), jnp.float32).at[dest].set(g_flat[order])
    nblk = rows // EXPERT_BLOCK
    blk_start = jnp.arange(nblk, dtype=jnp.int32) * EXPERT_BLOCK
    blk_exp = jnp.minimum(jnp.sum(pend[None, :] <= blk_start[:, None], axis=1), N_EXPERTS - 1)
    x_pad = jnp.concatenate([xt, jnp.zeros((1, d), xt.dtype)], axis=0)
    x_rows = x_pad[row_tok].reshape(nblk, EXPERT_BLOCK, d)

    def expert_block(args):
        xb, e = args
        gu = xb @ w_up_gate[e] + b_up_gate[e]
        gate = jnp.minimum(gu[:, :D_EXPERT], SWIGLU_LIMIT)
        up = jnp.clip(gu[:, D_EXPERT:], -SWIGLU_LIMIT, SWIGLU_LIMIT)
        act = (up + 1) * (gate * jax.nn.sigmoid(SWIGLU_ALPHA * gate))
        return act @ w_down[e] + b_down[e]

    y_rows = lax.map(expert_block, (x_rows, blk_exp)).reshape(rows, d)
    y = jax.ops.segment_sum(y_rows * row_gate[:, None].astype(y_rows.dtype), row_tok,
                            num_segments=n + 1)[:n]
    return y.reshape(b, s, d)

def setup_inputs(seed: int = 0) -> dict:
    key = jax.random.key(seed)
    ks = jax.random.split(key, 20)
    f32 = jnp.float32
    nrm = lambda k, shape, scale: jax.random.normal(k, shape, f32) * scale
    return {
        "x": nrm(ks[0], (BATCH, SEQ, D_MODEL), 1.0),
        "norm_mix": 1.0 + nrm(ks[1], (DEPTH, D_MODEL), 0.02),
        "w_in": nrm(ks[2], (DEPTH, D_MODEL, IN_WIDTH), D_MODEL ** -0.5),
        "b_forget": 2.0 + nrm(ks[3], (DEPTH, FOX_HEADS), 0.5),
        "q_norm_fox": 1.0 + nrm(ks[4], (DEPTH, HEAD_DIM), 0.02),
        "k_norm_fox": 1.0 + nrm(ks[5], (DEPTH, HEAD_DIM), 0.02),
        "q_norm_swa": 1.0 + nrm(ks[6], (DEPTH, HEAD_DIM), 0.02),
        "k_norm_swa": 1.0 + nrm(ks[7], (DEPTH, HEAD_DIM), 0.02),
        "sinks": nrm(ks[8], (DEPTH, SWA_HEADS), 0.5),
        "rel_bias": nrm(ks[9], (N_BUCKETS, SWA_HEADS), 0.5),
        "w_out": nrm(ks[10], (DEPTH, MIX_WIDTH, D_MODEL), MIX_WIDTH ** -0.5),
        "norm_moe": 1.0 + nrm(ks[11], (DEPTH, D_MODEL), 0.02),
        "w_router": nrm(ks[12], (DEPTH, D_MODEL, N_EXPERTS), D_MODEL ** -0.5),
        "b_router": nrm(ks[13], (DEPTH, N_EXPERTS), 0.01),
        "w_up_gate": nrm(ks[14], (DEPTH, N_EXPERTS, D_MODEL, 2 * D_EXPERT), D_MODEL ** -0.5),
        "b_up_gate": nrm(ks[15], (DEPTH, N_EXPERTS, 2 * D_EXPERT), 0.02),
        "w_down": nrm(ks[16], (DEPTH, N_EXPERTS, D_EXPERT, D_MODEL), D_EXPERT ** -0.5),
        "b_down": nrm(ks[17], (DEPTH, N_EXPERTS, D_MODEL), 0.02),
    }

def reference(x, norm_mix, w_in, b_forget, q_norm_fox, k_norm_fox, q_norm_swa, k_norm_swa,
              sinks, rel_bias, w_out, norm_moe, w_router, b_router, w_up_gate, b_up_gate,
              w_down, b_down):
    b, s, _ = x.shape
    points = [int(p) for p in np.cumsum(IN_SPLITS)[:-1]]
    h = x
    for l in range(DEPTH):
        hn = rms_norm(h, norm_mix[l])
        proj = hn @ w_in[l]
        qa, ka, va, fa, qb, kb, vb = jnp.split(proj, points, axis=-1)
        qa = rms_norm(qa.reshape(b, s, FOX_HEADS, HEAD_DIM), q_norm_fox[l])
        ka = rms_norm(ka.reshape(b, s, FOX_HEADS, HEAD_DIM), k_norm_fox[l])
        va = va.reshape(b, s, FOX_HEADS, HEAD_DIM)
        out_a = fox_attention(qa, ka, va, fa + b_forget[l])
        qb = rms_norm(qb.reshape(b, s, SWA_HEADS, HEAD_DIM), q_norm_swa[l])
        kb = rms_norm(kb.reshape(b, s, SWA_KV_HEADS, HEAD_DIM), k_norm_swa[l])
        vb = vb.reshape(b, s, SWA_KV_HEADS, HEAD_DIM)
        out_b = swa_sink_attention(qb, kb, vb, sinks[l], rel_bias)
        h = h + jnp.concatenate([out_a, out_b], axis=-1) @ w_out[l]
        h = h + moe_ffn(rms_norm(h, norm_moe[l]), w_router[l], b_router[l], w_up_gate[l],
                        b_up_gate[l], w_down[l], b_down[l])
    return h


_drawn_inputs = setup_inputs


def setup_inputs(seed=0):
    import zlib

    import numpy as np

    out = dict(_drawn_inputs(seed))
    spreads = {}
    factors = {'q_norm_fox': 3.084,
     'q_norm_swa': 3.711,
     'k_norm_swa': 5.235,
     'sinks': 35.122,
     'b_up_gate': 5.307,
     'b_down': 6.09}
    for name, (base, spread) in spreads.items():
        noise = np.random.default_rng([zlib.crc32(name.encode()), seed]).standard_normal(out[name].shape)
        drawn = base * np.exp(spread * noise) if base else spread * noise
        out[name] = __import__('jax').numpy.asarray(drawn.astype(out[name].dtype))
    for name, factor in factors.items():
        out[name] = (out[name] * factor).astype(out[name].dtype)
    return out
```

```python
from contextlib import ExitStack

import numpy as np

import concourse.bass as bass
from concourse import mybir

F32 = mybir.dt.float32
BF16 = mybir.dt.bfloat16
U32 = mybir.dt.uint32
I32 = mybir.dt.int32
ALU = mybir.AluOpType
ACT = mybir.ActivationFunctionType
AX = mybir.AxisListType

P = 128
SEQ = 512
D = 1024
TILES = SEQ // P
KT = D // P
HD = 64
HEADS = 8
KV = 2
GROUP = HEADS // KV
BUCKETS = 32
WINDOW = 128
MAX_DISTANCE = 128
EXPERTS = 32
TOPK = 4
LIMIT = 7.0
ALPHA = 1.702
EPS = 1e-6
NEG = -1e30
BAND = 2 * WINDOW
TOEP = 3 * WINDOW
HALF = 512
HW = HEADS * HD
IN_WIDTH = 4 * HW + HEADS + 2 * KV * HD
OUT_ROWS = SEQ + P
OVER = TOPK * SEQ // P - 1
CHUNKS = 12
CHUNK_COLS = 2 * D

QA, KA, VA, FG, QB, KB = 0, HW, 2 * HW, 3 * HW, 3 * HW + HEADS, 4 * HW + HEADS
CH = ["kvf", "ka", "va", "qa", "qb"]
CH_AT = {"ka": KA, "va": VA, "qa": QA, "qb": QB}
KVF = 2 * KV * HD + HEADS
NORMED = ["kvf", "ka", "qa", "qb"]


def later(t):
    return not (isinstance(t, int) and t == 0)


def bucket_table():
    table = np.zeros((BUCKETS + 1, TOEP), np.float32)
    for m in range(TOEP):
        n = 2 * WINDOW - 1 - m
        if not 0 <= n < WINDOW:
            table[BUCKETS, m] = NEG
            continue
        half = BUCKETS // 2
        if n < half:
            b = n
        else:
            large = np.log(np.float32(n) / np.float32(half)) / np.float32(np.log(MAX_DISTANCE / half))
            b = min(half + int(np.float32(large) * np.float32(BUCKETS - half)), BUCKETS - 1)
        table[b, m] = 1.0
    return table


def schedule():
    order = [("hn", t) for t in range(TILES)] + [("toep", h) for h in range(HEADS)]
    units = [(c, t) for c in CH for t in range(TILES)]
    for n, (c, t) in enumerate(units):
        order.append(("proj", c, t))
        if n >= 2 and units[n - 2][0] in NORMED:
            order.append(("turn", *units[n - 2]))
        if n == 9:
            order.append(("decay",))
        if n == 11:
            order.append(("decay_turn",))
    order += [("turn", *u) for u in units[-2:]]
    total = TILES * 2 * HEADS
    fill = {3: "mix", 5: "out0", 7: "out1", 11: "hn2", 13: "route"}
    order += [("score", 0), ("score", 1)]
    for g in range(total):
        order.append(("probs", g))
        if g + 2 < total:
            order.append(("score", g + 2))
        if g:
            order.append(("value", g - 1))
        if g >= 2 * HEADS and g % (2 * HEADS) in fill:
            order.append((fill[g % (2 * HEADS)], g // (2 * HEADS) - 1))
    order.append(("value", total - 1))
    order += [(fill[i], TILES - 1) for i in sorted(fill)]
    order.append(("place",))
    return order


def bank_plan(order):
    turns, accs = [], []
    for s in order:
        if s[0] in ("hn", "mix", "hn2"):
            turns += [(s, 0), (s, 1)]
        elif s[0] in ("toep", "turn", "decay", "decay_turn", "probs", "route", "place"):
            turns.append((s, 0))
        elif s[0] in ("proj", "out0", "out1"):
            accs.append((s, 0))
    return {k: (n % 2, n // 2) for n, k in enumerate(turns)}, {k: (n % 2, n // 2) for n, k in enumerate(accs)}


def layer_kernel(nc, x, norm_mix, w_in, b_forget, q_norm_fox, k_norm_fox, q_norm_swa, k_norm_swa, sinks,
                 rel_bias, w_out, norm_moe, w_router, b_router, w_up_gate, b_up_gate, w_down, b_down,
                 buckets, out):
    order = schedule()
    T, A = bank_plan(order)

    toep_dram = nc.dram_tensor("toeplitz_rows", [P, HEADS * TOEP], F32, kind="Internal").ap()
    hn2_dram = nc.dram_tensor("normed_rows", [SEQ, D], F32, kind="Internal").ap()

    ctx = ExitStack()
    with ctx:
        def sb(name, shape, dt=F32, at=ctx):
            return at.enter_context(nc.sbuf_tensor(name, shape, dt))

        def sem(name):
            return ctx.enter_context(nc.semaphore(name))

        ring = sb("ring", [P, CHUNKS * CHUNK_COLS])
        ident = sb("ident", [P, P])
        ident_b = sb("ident_b", [P, P], BF16)
        ones_b = sb("ones_b", [P, P], BF16)
        before = sb("before", [P, P], BF16)
        iota_slot = sb("iota_slot", [P, SEQ])
        iota_exp = sb("iota_exp", [P, EXPERTS])
        lane = sb("lane", [P, 1])
        slot_trash = sb("slot_trash", [P, 1])
        gate_parts = sb("gate_parts", [P, TILES, EXPERTS, 3], BF16)
        posm = sb("posm", [P, TILES, EXPERTS])
        bias_tab = sb("bias_tab", [96, 3 * D], BF16)
        expert_row = sb("expert_row", [96, EXPERTS], BF16)
        over_tab = sb("over_tab", [1, 3 * 16], I32)

        early = ExitStack()
        qaT = sb("qaT", [P, 4, SEQ], at=early)
        kaT = sb("kaT", [P, 4, SEQ], at=early)
        qbT = sb("qbT", [P, 4, SEQ], at=early)
        kbT = sb("kbT", [P, KV, SEQ], at=early)
        va = sb("va", [P, TILES, HW], at=early)
        vb = sb("vb", [P, TILES, KV * HD], at=early)
        swa_bias = sb("swa_bias", [P, HEADS, BAND], at=early)
        causal = sb("causal", [P, SEQ], at=early)
        s_sb = sb("s_sb", [P, 2, HALF], at=early)
        p_sb = sb("p_sb", [P, 2, HALF], at=early)
        pT = sb("pT", [P, 2, HALF], at=early)
        cT = sb("cT", [24, SEQ], BF16, at=early)
        ncT = sb("ncT", [24, SEQ], BF16, at=early)
        head_row = sb("head_row", [24, HEADS, P], BF16, at=early)
        gcols = sb("gcols", [P, 4], at=early)
        gmix = sb("gmix", [P, KT], at=early)
        bf_b = sb("bf_b", [P, HEADS], at=early)
        sink_b = sb("sink_b", [P, HEADS], at=early)
        nsink = sb("nsink", [P, HEADS], at=early)
        br_b = sb("br_b", [P, EXPERTS], at=early)
        wr = sb("wr", [P, KT, EXPERTS], at=early)
        rel = sb("rel", [BUCKETS + 1, HEADS], at=early)
        ss = sb("ss", [P, 8], at=early)
        rs = sb("rs", [P, 8], at=early)
        eps_d = sb("eps_d", [P, 1], at=early)
        eps_h = sb("eps_h", [P, 1], at=early)
        ssx = sb("ssx", [P, TILES], at=early)
        rsx = sb("rsx", [P, TILES], at=early)
        zf = sb("zf", [P, TILES, HEADS], at=early)
        za = sb("za", [P, TILES, HEADS], at=early)
        ze = sb("ze", [P, TILES, HEADS], at=early)
        logf = sb("logf", [P, TILES, HEADS], at=early)
        tri = sb("tri", [P, P], at=early)
        ones = sb("ones", [P, P], at=early)
        csum = sb("csum", [P, TILES, HEADS], at=early)
        crest = sb("crest", [P, TILES, HEADS], at=early)
        cpart = sb("cpart", [P, TILES, 3, HEADS], BF16, at=early)
        negm = sb("negm", [P, 2, 2 * HEADS], at=early)
        den = sb("den", [P, 2, 2 * HEADS], at=early)
        sk = sb("sk", [P, 2, HEADS], at=early)
        rden = sb("rden", [P, 2 * HEADS], at=early)
        lg = sb("lg", [P, EXPERTS], at=early)
        top = sb("top", [P, 8], at=early)
        topi = sb("topi", [P, 8], U32, at=early)
        topf = sb("topf", [P, TOPK], at=early)
        ntop = sb("ntop", [P, 1], at=early)
        ex = sb("ex", [P, TOPK], at=early)
        exs = sb("exs", [P, 2], at=early)
        eq = sb("eq", [P, TOPK, EXPERTS], at=early)
        eqg = sb("eqg", [P, TOPK, EXPERTS], at=early)
        gsum = sb("gsum", [P, EXPERTS], at=early)
        mask = sb("mask", [P, TILES, EXPERTS], at=early)
        mask_b = sb("mask_b", [P, TILES, EXPERTS], BF16, at=early)
        ss2 = sb("ss2", [P, 2], at=early)

        proj_mem = ExitStack()
        hnT = sb("hnT", [P, KT, SEQ], at=proj_mem)
        xt = sb("xt", [P, 2, D], at=proj_mem)
        qn = sb("qn", [P, 2, HW], at=proj_mem)
        sq = sb("sq", [P, HW], at=proj_mem)
        proj_mem.close()
        tail_mem = ExitStack()
        o_sb = sb("o_sb", [P, D], at=tail_mem)
        mixT = sb("mixT", [P, KT, P], at=tail_mem)
        hb = sb("hb", [P, D], at=tail_mem)
        hn2 = sb("hn2", [P, D], at=tail_mem)
        hn2T = sb("hn2T", [P, KT, P], at=tail_mem)
        gmoe = sb("gmoe", [P, D], at=tail_mem)
        tail_mem.close()
        early.close()

        late = ExitStack()
        gx = sb("gx", [P, D], at=late)
        xT = sb("xT", [P, KT, P], at=late)
        gmin = sb("gmin", [P, D], at=late)
        sig = sb("sig", [P, D], at=late)
        gs = sb("gs", [P, D], at=late)
        up = sb("up", [P, D], at=late)
        act_sb = sb("act_sb", [P, D], at=late)
        actT = sb("actT", [P, KT, P], at=late)
        y_sb = sb("y_sb", [P, D], at=late)
        iota_blk = sb("iota_blk", [P, P], at=late)
        poscol = sb("poscol", [P, TILES], at=late)
        slot_oh = sb("slot_oh", [P, TILES, P], BF16, at=late)
        idx_rhs = sb("idx_rhs", [P, TILES, 5], BF16, at=late)
        bias_sel = sb("bias_sel", [96, P], BF16, at=late)
        tokf = sb("tokf", [P, 1], at=late)
        gidx = sb("gidx", [P, 1], U32, at=late)
        sidx_next = sb("sidx_next", [P, 1], at=late)
        gate_next = sb("gate_next", [P, 1], at=late)
        sidx = sb("sidx", [P, 1], U32, at=late)
        gate = sb("gate", [P, 1], at=late)
        btmp = sb("btmp", [96, 3 * D], at=late)
        ocnt = sb("ocnt", [32, 1], at=late)
        oext = sb("oext", [32, 1], at=late)
        oext_b = sb("oext_b", [32, 1], BF16, at=late)
        ostart = sb("ostart", [32, 1], at=late)
        odif = sb("odif", [32, 16], at=late)
        ooh = sb("ooh", [32, 3, 16], at=late)
        ones_f = sb("ones_f", [32, P], at=late)
        late.close()

        w_buf = [ring[:, (8 + 2 * b) * CHUNK_COLS:(10 + 2 * b) * CHUNK_COLS].rearrange("p (k n) -> p k n", k=KT)
                 for b in range(2)]
        wout_sb = ring[:, 8 * CHUNK_COLS:12 * CHUNK_COLS].rearrange("p (k n) -> p k n", k=KT)
        toep_sb = ring[:, 6 * CHUNK_COLS:6 * CHUNK_COLS + HEADS * TOEP]
        lams = ring[0:BUCKETS + 1, 4 * CHUNK_COLS:4 * CHUNK_COLS + HEADS * P].rearrange("b (h p) -> b h p", p=P)
        tabs = ring[0:BUCKETS + 1, 5 * CHUNK_COLS:5 * CHUNK_COLS + TOEP]

        banks = [ctx.enter_context(nc.psum_tensor(f"bank{i}", [P, HALF], F32)) for i in range(8)]
        acc_ps, s_ps, t_ps, o_ps = banks[0:2], banks[2:4], banks[4:6], banks[6:8]
        gate_ps, up_ps, y_ps, turn_ps = banks[0:2], banks[2:4], banks[6:8], banks[4:6]

        x_loaded = [sem(f"x_loaded{i}") for i in range(2)]
        small_loaded = sem("small_loaded")
        tail_loaded = sem("tail_loaded")
        win_loaded = [sem(f"win_loaded{i}") for i in range(2)]
        wout_loaded = sem("wout_loaded")
        consts = sem("consts")
        masks_built = sem("masks_built")
        toep_stored = sem("toep_stored")
        bias_loaded = sem("bias_loaded")
        xn_sq = sem("xn_sq")
        xn_ready = sem("xn_ready")
        eps_ready = sem("eps_ready")
        rs_ready = sem("rs_ready")
        gcols_ready = sem("gcols_ready")
        lams_ready = sem("lams_ready")
        ct_ready = sem("ct_ready")
        sink_in = sem("sink_in")
        va_ready = sem("va_ready")
        vb_ready = sem("vb_ready")
        zf_ready = sem("zf_ready")
        t_full = [sem(f"t_full{i}") for i in range(2)]
        t_free = [sem(f"t_free{i}") for i in range(2)]
        a_full = [sem(f"a_full{i}") for i in range(2)]
        sq_ready = sem("sq_ready")
        sq_free = sem("sq_free")
        qn_ready = sem("qn_ready")
        f_ready = sem("f_ready")
        f_log = sem("f_log")
        logf_ready = sem("logf_ready")
        cpart_ready = sem("cpart_ready")
        score_ready = sem("score_ready")
        score_done = sem("score_done")
        probs_ready = sem("probs_ready")
        value_done = sem("value_done")
        sink_exp = sem("sink_exp")
        mix_ready = sem("mix_ready")
        h_in = sem("h_in")
        h_ready = sem("h_ready")
        h_sq = sem("h_sq")
        hn2_ready = sem("hn2_ready")
        rows_stored = sem("rows_stored")
        hn2_turned = sem("hn2_turned")
        ntop_ready = sem("ntop_ready")
        ex_ready = sem("ex_ready")
        mask_ready = sem("mask_ready")
        step = sem("step")
        placed = sem("placed")
        w_loaded = [sem(f"w_loaded{c}") for c in range(CHUNKS)]
        chunk_used = sem("chunk_used")
        late_consts = sem("late_consts")
        bias_raw = sem("bias_raw")
        bias_ready = sem("bias_ready")
        over_step = sem("over_step")
        over_pe = sem("over_pe")
        over_ready = sem("over_ready")
        cols_copied = sem("cols_copied")
        onehot_ready = sem("onehot_ready")
        idx_psum = sem("idx_psum")
        idx_sum = sem("idx_sum")
        idx_ready = sem("idx_ready")
        cur_ready = sem("cur_ready")
        gathered = sem("gathered")
        x_transposed = sem("x_transposed")
        xT_ready = sem("xT_ready")
        sel_ready = sem("sel_ready")
        gate_psum = sem("gate_psum")
        up_psum = sem("up_psum")
        gmin_ready = sem("gmin_ready")
        sig_ready = sem("sig_ready")
        gs_ready = sem("gs_ready")
        up_ready = sem("up_ready")
        act_ready = sem("act_ready")
        act_transposed = sem("act_transposed")
        actT0_ready = sem("actT0_ready")
        actT1_ready = sem("actT1_ready")
        y_psum = sem("y_psum")
        y_ready = sem("y_ready")
        scattered = sem("scattered")

        def t_filled(eng, key, half=0):
            b, n = T[(key, half)]
            eng.wait_ge(t_full[b], n + 1)
            return b

        def t_evacuated(eng, key, half=0):
            b, n = T[(key, half)]
            eng.wait_ge(t_free[b], n + 1)

        def head_of(i):
            h = i % HEADS
            return i < HEADS, h, h // 2, HD * (h % 2)

        def keys_of(g):
            t, fox = g // 16, g % 16 < HEADS
            first = 0 if fox or t == 0 else t - 1
            return first, t + 1 - first

        block = ctx.enter_context(nc.Block())

        @block.sync
        def _(sp):
            def load_small(dst, src):
                sp.dma_start(dst, src, allow_slow_non_contiguous=True).then_inc(small_loaded, 16)

            def load_x(t):
                if t >= 2:
                    t_filled(sp, ("hn", t - 2), 1)
                sp.dma_start(xt[:, t % 2, :], x[0, t * P:(t + 1) * P, :]).then_inc(x_loaded[t % 2], 16)

            def load_win(n):
                c = CH[n]
                if n >= 2:
                    b, k = A[(("proj", CH[n - 2], TILES - 1), 0)]
                    sp.wait_ge(a_full[b], k + 1)
                dst = w_buf[n % 2]
                if c == "kvf":
                    sp.dma_start(dst[:, :, 0:2 * KV * HD], w_in[0, :, KB:IN_WIDTH].rearrange("(k p) n -> p k n", p=P)
                                 ).then_inc(win_loaded[0], 16)
                    sp.dma_start(dst[:, :, 2 * KV * HD:KVF], w_in[0, :, FG:QB].rearrange("(k p) n -> p k n", p=P)
                                 ).then_inc(win_loaded[0], 16)
                else:
                    sp.dma_start(dst, w_in[0, :, CH_AT[c]:CH_AT[c] + HW].rearrange("(k p) n -> p k n", p=P)
                                 ).then_inc(win_loaded[n % 2], 16)

            load_x(0)
            load_x(1)
            load_small(gmix[:, :], norm_mix[0].rearrange("(k p) -> p k", p=P))
            for j, g in enumerate((q_norm_fox, k_norm_fox, q_norm_swa, k_norm_swa)):
                for half in range(2):
                    load_small(gcols[half * HD:(half + 1) * HD, j:j + 1], g.rearrange("a d -> d a"))
            load_small(bf_b[:, :], b_forget.broadcast_to([P, HEADS]))
            load_small(sink_b[:, :], sinks.broadcast_to([P, HEADS]))
            load_small(br_b[:, :], b_router.broadcast_to([P, EXPERTS]))
            load_small(wr[:, :, :], w_router[0].rearrange("(k p) n -> p k n", p=P))
            load_small(rel[0:BUCKETS, :], rel_bias)
            load_small(tabs, buckets)
            load_win(0)
            load_x(2)
            load_x(3)
            load_win(1)
            sp.wait_ge(t_free[T[(("toep", HEADS - 2), 0)][0]], T[(("toep", HEADS - 2), 0)][1] + 1)
            sp.wait_ge(t_free[T[(("toep", HEADS - 1), 0)][0]], T[(("toep", HEADS - 1), 0)][1] + 1)
            sp.dma_start(toep_dram, toep_sb).then_inc(toep_stored, 16)
            sp.wait_ge(toep_stored, 16)
            row = HEADS * TOEP
            skew = toep_dram.rearrange("p c -> (p c)")[WINDOW - 1:WINDOW - 1 + P * (row - 1)]
            skew = skew.rearrange("(q c) -> q c", c=row - 1)
            for h in range(HEADS):
                sp.dma_start(swa_bias[:, h, :], skew[:, h * TOEP:h * TOEP + BAND]).then_inc(bias_loaded, 16)
            def load_chunk(c, e):
                dst = ring[:, c * CHUNK_COLS:(c + 1) * CHUNK_COLS].rearrange("p (k n) -> p k n", k=2)
                k = c % 4
                if c < 8:
                    src = w_up_gate[0, e, k * 2 * P:(k + 1) * 2 * P, (c // 4) * D:(c // 4 + 1) * D]
                else:
                    src = w_down[0, e, k * 2 * P:(k + 1) * 2 * P, :]
                return dst, src.rearrange("(k p) n -> p k n", p=P)

            load_win(2)
            for c in range(8):
                sp.dma_start(*load_chunk(c, 0)).then_inc(w_loaded[c], 16)
            load_win(3)
            load_win(4)
            for n in (3, 4):
                b, k = A[(("proj", CH[n], TILES - 1), 0)]
                sp.wait_ge(a_full[b], k + 1)
            sp.dma_start(wout_sb, w_out[0].rearrange("(k p) n -> p k n", p=P)).then_inc(wout_loaded, 16)
            t_filled(sp, ("turn", "qb", TILES - 1))
            sp.dma_start(gmoe[:, :], norm_moe.broadcast_to([P, D])).then_inc(tail_loaded, 16)
            for t in range(TILES):
                if t:
                    sp.wait_ge(rows_stored, 32 * t)
                    sp.wait_ge(hn2_ready, t)
                sp.dma_start(hb[:, :], x[0, t * P:(t + 1) * P, :]).then_inc(h_in, 16)
                sp.wait_ge(h_ready, 2 * t + 2)
                sp.dma_start(out[t * P:(t + 1) * P, :], hb[:, :]).then_inc(rows_stored, 16)
                sp.wait_ge(hn2_ready, t + 1)
                sp.dma_start(hn2_dram[t * P:(t + 1) * P, :], hn2[:, :]).then_inc(rows_stored, 16)
            sp.dma_start(out[SEQ:OUT_ROWS, :], hn2[:, :]).then_inc(rows_stored, 16)
            b, k = A[(("out1", TILES - 1), 0)]
            sp.wait_ge(a_full[b], k + 1)
            for c in range(8, CHUNKS):
                sp.dma_start(*load_chunk(c, 0)).then_inc(w_loaded[c], 16)
            sp.wait_ge(placed, 1)
            for r in range(3):
                sp.dma_start(btmp[32 * r:32 * r + 32, 0:2 * D], b_up_gate[0]).then_inc(bias_raw, 16)
                sp.dma_start(btmp[32 * r:32 * r + 32, 2 * D:3 * D], b_down[0]).then_inc(bias_raw, 16)

            with sp.Fori(1, EXPERTS) as e:
                for c in range(CHUNKS):
                    sp.wait_ge(chunk_used, e * CHUNKS - (CHUNKS - c - 1))
                    sp.dma_start(*load_chunk(c, e)).then_inc(w_loaded[c], 16)
            sp.wait_ge(over_ready, 1)
            with sp.Fori(0, OVER) as j:
                used = sp.value_load(over_tab[0:1, bass.ds(j + 32, 1)], min_val=0, max_val=1)
                with sp.If(used > 0):
                    e = sp.value_load(over_tab[0:1, bass.ds(j, 1)], min_val=0, max_val=EXPERTS - 1)
                    for c in range(CHUNKS):
                        sp.wait_ge(chunk_used, (j + EXPERTS) * CHUNKS - (CHUNKS - c - 1))
                        sp.dma_start(*load_chunk(c, e)).then_inc(w_loaded[c], 16)

        @block.gpsimd
        def _(pool):
            g = nc.gpsimd
            for dst, v in ((ident, 0.0), (ident_b, 0.0), (ones, 1.0), (ones_b, 1.0), (tri, 1.0), (before, 1.0),
                           (causal, 0.0), (expert_row, 0.0)):
                g.memset(dst[:, :], v).then_inc(consts, 1)
            g.memset(head_row[:, :, :], 0.0).then_inc(consts, 1)
            g.iota(iota_slot[:, :], pattern=[[1, SEQ]], base=0, channel_multiplier=0,
                   allow_small_or_imprecise_dtypes=True).then_inc(consts, 1)
            g.iota(iota_exp[:, :], pattern=[[1, EXPERTS]], base=0, channel_multiplier=0,
                   allow_small_or_imprecise_dtypes=True).then_inc(consts, 1)
            g.iota(lane[:, :], pattern=[[0, 1]], base=0, channel_multiplier=1,
                   allow_small_or_imprecise_dtypes=True).then_inc(consts, 1)
            g.iota(slot_trash[:, :], pattern=[[0, 1]], base=SEQ, channel_multiplier=1,
                   allow_small_or_imprecise_dtypes=True).then_inc(consts, 1)
            pool.wait_ge(consts, 13)
            for m in (ident, ident_b):
                g.affine_select(out=m[:, :], in_=m[:, :], compare_op=ALU.not_equal, fill=1.0, base=0,
                                pattern=[[-1, P]], channel_multiplier=1).then_inc(masks_built, 1)
            g.affine_select(out=tri[:, :], in_=tri[:, :], compare_op=ALU.is_ge, fill=0.0, base=0,
                            pattern=[[1, P]], channel_multiplier=-1).then_inc(masks_built, 1)
            g.affine_select(out=before[:, :], in_=before[:, :], compare_op=ALU.is_ge, fill=0.0, base=-1,
                            pattern=[[1, P]], channel_multiplier=-1).then_inc(masks_built, 1)
            dia = causal[:, SEQ - P:SEQ]
            g.affine_select(out=dia, in_=dia, compare_op=ALU.is_ge, fill=NEG, base=0,
                            pattern=[[-1, P]], channel_multiplier=1).then_inc(masks_built, 1)
            for part in range(3):
                g.affine_select(out=head_row[:, :, :], in_=head_row[:, :, :], compare_op=ALU.not_equal, fill=1.0,
                                base=-8 * part, pattern=[[-1, HEADS], [0, P]], channel_multiplier=1
                                ).then_inc(masks_built, 1)
                g.affine_select(out=expert_row[:, :], in_=expert_row[:, :], compare_op=ALU.not_equal, fill=1.0,
                                base=-32 * part, pattern=[[-1, EXPERTS]], channel_multiplier=1
                                ).then_inc(masks_built, 1)
                pool.wait_ge(masks_built, 5 + 2 * (part + 1))

            pool.wait_ge(placed, 1)
            g.memset(gx[:, :], 0.0).then_inc(late_consts, 1)
            g.memset(ones_f[:, :], 1.0).then_inc(late_consts, 1)
            g.tensor_copy(iota_blk[:, :], iota_slot[:, 0:P]).then_inc(late_consts, 1)
            for j in range(TILES):
                g.memset(idx_rhs[:, j, 0:1], float(P * j - 1024)).then_inc(late_consts, 1)
                g.tensor_copy(idx_rhs[:, j, 1:2], lane[:, :]).then_inc(late_consts, 1)
            pool.wait_ge(late_consts, 3 + 2 * TILES)

            def value(n):
                return n if isinstance(n, int) else pool.to_reg(n)

            def columns(s, e):
                if later(s):
                    pool.wait_ge(idx_psum, s)
                g.tensor_copy(poscol[:, :].unsqueeze(2), posm[:, :, bass.ds(e, 1)]).then_inc(cols_copied, 1)
                g.tensor_copy(idx_rhs[:, :, 2:5].unsqueeze(2), gate_parts[:, :, bass.ds(e, 1), :]
                              ).then_inc(cols_copied, 1)
                copied = value(2 * s + 2)
                pool.wait_ge(consts, 13)
                pool.wait_ge(cols_copied, copied)
                for j in range(TILES):
                    last = g.tensor_scalar(slot_oh[:, j, :], iota_blk[:, :], poscol[:, j:j + 1], None, ALU.is_equal)
                    last.then_inc(onehot_ready, 1)

            def gather(s):
                pool.wait_ge(consts, 13)
                pool.wait_ge(idx_ready, s * 2 + 2)
                if later(s):
                    pool.wait_ge(x_transposed, s)
                pool.indirect_dma_start(
                    out=gx[:, :], out_offset=None, in_=hn2_dram,
                    in_offset=bass.IndirectOffsetOnAxis(ap=gidx[:, 0:1], axis=0),
                    bounds_check=SEQ - 1, oob_is_err=False).then_inc(gathered, 16)

            def select_bias(t, e):
                if later(t):
                    pool.wait_ge(y_psum, t)
                g.tensor_copy(bias_sel[:, :], expert_row[:, bass.ds(e, 1)].broadcast_to([96, P])
                              ).then_inc(sel_ready, 1)

            def scatter(t):
                results, current, before_it = value(t + 1), value(2 * t + 2), value(t * 16)
                pool.wait_ge(consts, 13)
                pool.wait_ge(y_ready, results)
                pool.wait_ge(cur_ready, current)
                if later(t):
                    pool.wait_ge(scattered, before_it)
                pool.indirect_dma_start(
                    out=out, out_offset=bass.IndirectOffsetOnAxis(ap=sidx[:, 0:1], axis=0),
                    in_=y_sb[:, :], in_offset=None, compute_op=ALU.add).then_inc(scattered, 16)

            columns(0, 0)
            pool.wait_ge(rows_stored, 16 * (2 * TILES + 1))
            gather(0)
            select_bias(0, 0)
            columns(1, 1)
            gather(1)
            scatter(0)
            with pool.Fori(1, EXPERTS - 1) as t:
                select_bias(t, t)
                columns(t + 1, t + 1)
                gather(t + 1)
                scatter(t)
            select_bias(EXPERTS - 1, EXPERTS - 1)
            scatter(EXPERTS - 1)
            pool.wait_ge(scattered, 16 * EXPERTS)
            pool.wait_ge(over_ready, 1)
            with pool.Fori(0, OVER) as j:
                used = pool.value_load(over_tab[0:1, bass.ds(j + 32, 1)], min_val=0, max_val=1)
                with pool.If(used > 0):
                    e = pool.value_load(over_tab[0:1, bass.ds(j, 1)], min_val=0, max_val=EXPERTS - 1)
                    rank = pool.value_load(over_tab[0:1, bass.ds(j + 16, 1)], min_val=0, max_val=TILES - 1)
                    t = j + EXPERTS
                    pool.wait_ge(idx_psum, t)
                    g.tensor_copy(iota_blk[:, :], iota_slot[:, bass.ds(rank * P, P)]).then_inc(late_consts, 1)
                    pool.wait_ge(late_consts, j + (4 + 2 * TILES))
                    columns(t, e)
                    gather(t)
                    select_bias(t, e)
                    scatter(t)
                    pool.wait_ge(scattered, t * 16 + 16)

        @block.scalar
        def _(act):
            a = nc.scalar

            def root(dst, src, eps):
                a.activation(dst, src, ACT.Sqrt, bias=eps).then_inc(rs_ready, 1)

            act.wait_ge(eps_ready, 2)

            def hn(t):
                act.wait_ge(x_loaded[t % 2], 16 * (t // 2 + 1))
                a.activation(s_sb[:, :, :].rearrange("p a n -> p (a n)"), xt[:, t % 2, :], ACT.Square,
                             accum_out=ssx[:, t:t + 1]).then_inc(xn_sq, 1)
                act.wait_ge(xn_sq, t + 1)
                root(rsx[:, t:t + 1], ssx[:, t:t + 1], eps_d[:, :])

            def proj(c, t):
                unit = CH.index(c) * TILES + t
                b, k = A[(("proj", c, t), 0)]
                act.wait_ge(a_full[b], k + 1)
                if c == "va":
                    a.copy(va[:, t, :], acc_ps[b][:, :]).then_inc(va_ready, 1)
                    return
                n = NORMED.index(c) * TILES + t
                w = HW if c != "kvf" else KV * HD
                if n:
                    act.wait_ge(sq_free, n)
                a.activation(sq[:, 0:w], acc_ps[b][:, 0:w], ACT.Square).then_inc(sq_ready, 1)
                heads = HEADS if c != "kvf" else KV
                act.wait_ge(sq_free, n + 1)
                root(rs[:, 0:heads], ss[:, 0:heads], eps_h[:, :])

            def turn(c, t):
                b = t_filled(act, ("turn", c, t))
                cols = slice(t * P, (t + 1) * P)
                dst, j, m = {"qa": (qaT, 0, 4), "ka": (kaT, 1, 4), "qb": (qbT, 2, 4), "kvf": (kbT, 3, 2)}[c]
                act.wait_ge(gcols_ready, 2)
                a.activation(dst[:, :, cols], t_ps[b][:, 0:m * P].rearrange("p (m n) -> p m n", m=m), ACT.Copy,
                             scale=gcols[:, j:j + 1]).then_inc(t_free[b], 1)

            def decay():
                act.wait_ge(f_ready, 1)
                a.activation(ze[:, :, :], za[:, :, :], ACT.Exp, scale=-1.0).then_inc(f_log, 1)
                act.wait_ge(f_log, 1)
                a.activation(ze[:, :, :], ze[:, :, :], ACT.Ln, bias=1.0).then_inc(f_log, 1)

            def score(g):
                t, i = divmod(g, 16)
                _, n = keys_of(g)
                act.wait_ge(score_ready, g + 1)
                if g >= 2:
                    t_filled(act, ("probs", g - 2))
                if i == 0 and t >= 2:
                    act.wait_ge(mix_ready, 2 * t - 2)
                a.activation(p_sb[:, g % 2, 0:n * P], s_sb[:, g % 2, 0:n * P], ACT.Exp, scale=-1.0,
                             bias=negm[:, t % 2, i:i + 1], accum_out=den[:, t % 2, i:i + 1]).then_inc(probs_ready, 1)

            def probs(g):
                if g % 2 == 0:
                    return
                _, n = keys_of(g)
                b = t_filled(act, ("probs", g))
                if g >= 2:
                    act.wait_ge(value_done, g - 1)
                a.copy(pT[:, g % 2, 0:n * P], t_ps[b][:, 0:n * P]).then_inc(t_free[b], 1)

            def value(g):
                t, i = divmod(g, 16)
                if i == 15:
                    act.wait_ge(sink_in, t + 1)
                    a.activation(sk[:, 1, :], sk[:, 0, :], ACT.Exp).then_inc(sink_exp, 1)

            def mix(t):
                b = t_filled(act, ("mix", t), 1)
                a.copy(mixT[:, 4:8, :], t_ps[b][:, :].rearrange("p (m n) -> p m n", m=4)).then_inc(t_free[b], 1)

            def out1(t):
                act.wait_ge(h_ready, 2 * t + 2)
                if t:
                    act.wait_ge(rows_stored, 32 * t)
                    t_filled(act, ("hn2", t - 1), 1)
                a.activation(hn2[:, :], hb[:, :], ACT.Square, accum_out=ss2[:, 0:1]).then_inc(h_sq, 1)
                act.wait_ge(h_sq, t + 1)
                root(ss2[:, 1:2], ss2[:, 0:1], eps_d[:, :])

            def hn2_(t):
                b = t_filled(act, ("hn2", t), 1)
                a.copy(hn2T[:, 4:8, :], t_ps[b][:, :].rearrange("p (m n) -> p m n", m=4)).then_inc(t_free[b], 1)

            def route(t):
                act.wait_ge(ntop_ready, t + 1)
                a.activation(ex[:, :], top[:, 0:TOPK], ACT.Exp, bias=ntop[:, :], accum_out=exs[:, 0:1]
                             ).then_inc(ex_ready, 1)

            does = {"hn": hn, "proj": proj, "turn": turn, "decay": decay, "score": score, "probs": probs,
                    "value": value, "mix": mix, "out1": out1, "hn2": hn2_, "route": route}
            for s in order:
                if s[0] in does:
                    does[s[0]](*s[1:])

            def rows_in(s):
                act.wait_ge(x_transposed, s + 1)
                for half in range(2):
                    a.copy(xT[:, 4 * half:4 * half + 4, :], y_ps[half][:, :].rearrange("p (m n) -> p m n", m=4)
                           ).then_inc(xT_ready, 1)

            def expert(t, ahead):
                act.wait_ge(gmin_ready, t + 1)
                if later(t):
                    act.wait_ge(gs_ready, t)
                a.activation(sig[:, :], gmin[:, :], ACT.Sigmoid, scale=ALPHA).then_inc(sig_ready, 1)
                if ahead:
                    rows_in(t + 1)
                act.wait_ge(act_transposed, t * 2 + 1)
                if later(t):
                    act.wait_ge(y_psum, t)
                a.copy(actT[:, 0:4, :], turn_ps[0][:, :].rearrange("p (m n) -> p m n", m=4)
                       ).then_inc(actT0_ready, 1)
                act.wait_ge(y_psum, t + 1)
                act.wait_ge(cur_ready, t * 2 + 2)
                if later(t):
                    act.wait_ge(scattered, t * 16)
                for half in range(2):
                    last = a.activation(y_sb[:, half * HALF:(half + 1) * HALF], y_ps[half][:, :], ACT.Copy,
                                        scale=gate[:, 0:1])
                last.then_inc(y_ready, 1)

            rows_in(0)
            expert(0, True)
            with act.Fori(1, EXPERTS - 1) as t:
                expert(t, True)
            expert(EXPERTS - 1, False)
            act.wait_ge(over_ready, 1)
            with act.Fori(0, OVER) as j:
                used = act.value_load(over_tab[0:1, bass.ds(j + 32, 1)], min_val=0, max_val=1)
                with act.If(used > 0):
                    rows_in(j + EXPERTS)
                    expert(j + EXPERTS, False)

        @block.vector
        def _(dve):
            v = nc.vector
            steps = [0]

            def link(ins):
                ins.then_inc(step, 1)
                steps[0] += 1
                dve.wait_ge(step, steps[0])

            v.memset(eps_d[:, :], D * EPS).then_inc(eps_ready, 1)
            v.memset(eps_h[:, :], HD * EPS).then_inc(eps_ready, 1)

            def hn(t):
                dve.wait_ge(rs_ready, t + 1)
                link(v.reciprocal(rsx[:, t:t + 1], rsx[:, t:t + 1]))
                v.tensor_scalar(xt[:, t % 2, :], xt[:, t % 2, :], rsx[:, t:t + 1], None, ALU.mult).then_inc(xn_ready, 1)
                if t == 0:
                    dve.wait_ge(small_loaded, 16 * 15)
                    link(v.tensor_scalar(gmix[:, :], gmix[:, :], D ** 0.5, None, ALU.mult))
                for half in range(2):
                    b = t_filled(dve, ("hn", t), half)
                    v.tensor_tensor(hnT[:, 4 * half:4 * half + 4, t * P:(t + 1) * P],
                                    t_ps[b][:, :].rearrange("p (m n) -> p m n", m=4),
                                    gmix[:, 4 * half:4 * half + 4].unsqueeze(2).broadcast_to([P, 4, P]),
                                    ALU.mult).then_inc(t_free[b], 1)
                if t == 0:
                    for j in (1, 3):
                        v.tensor_scalar(gcols[:, j:j + 1], gcols[:, j:j + 1], HD ** 0.5, None, ALU.mult
                                        ).then_inc(gcols_ready, 1)
                    v.tensor_scalar(nsink[:, :], sink_b[:, :], -1.0, None, ALU.mult).then_inc(step, 1)
                    steps[0] += 1
                    dve.wait_ge(consts, 13)
                    link(v.memset(rel[BUCKETS:BUCKETS + 1, :], 1.0))
                    v.tensor_copy(lams, rel[:, :].unsqueeze(2).broadcast_to([BUCKETS + 1, HEADS, P])
                                  ).then_inc(lams_ready, 1)

            def toep(h):
                b = t_filled(dve, ("toep", h))
                v.tensor_copy(toep_sb[:, h * TOEP:(h + 1) * TOEP], t_ps[b][:, 0:TOEP]).then_inc(t_free[b], 1)

            def proj(c, t):
                if c == "va":
                    return
                b, k = A[(("proj", c, t), 0)]
                n = NORMED.index(c) * TILES + t
                hn_ = HEADS if c != "kvf" else KV
                w = hn_ * HD
                dve.wait_ge(sq_ready, n + 1)
                v.tensor_reduce(ss[:, 0:hn_], sq[:, 0:w].rearrange("p (h d) -> p h d", d=HD), AX.X, ALU.add
                                ).then_inc(sq_free, 1)
                dve.wait_ge(rs_ready, TILES + n + 1)
                link(v.reciprocal(rs[:, 0:hn_], rs[:, 0:hn_]))
                if n >= 2:
                    c2, t2 = NORMED[(n - 2) // TILES], (n - 2) % TILES
                    t_filled(dve, ("turn", c2, t2))
                src = acc_ps[b][:, 0:w].rearrange("p (h d) -> p h d", d=HD)
                r = rs[:, 0:hn_].unsqueeze(2).broadcast_to([P, hn_, HD])
                if c == "kvf":
                    dst = qn[:, n % 2, 0:2 * w].rearrange("p (h u d) -> p u h d", u=2, d=HD)
                    v.tensor_tensor(dst[:, 0, :, :], src, r, ALU.mult).then_inc(qn_ready, 1)
                    v.tensor_tensor(dst[:, 1, :, :], src, r, ALU.mult).then_inc(qn_ready, 1)
                    v.tensor_copy(vb[:, t, :], acc_ps[b][:, KV * HD:2 * KV * HD]).then_inc(vb_ready, 1)
                    v.tensor_tensor(zf[:, t, :], acc_ps[b][:, 2 * KV * HD:KVF], bf_b[:, :], ALU.add
                                    ).then_inc(zf_ready, 1)
                    if t == TILES - 1:
                        dve.wait_ge(zf_ready, TILES)
                        link(v.tensor_scalar(za[:, :, :], zf[:, :, :], -1.0, None, ALU.mult))
                        v.tensor_tensor(za[:, :, :], za[:, :, :], zf[:, :, :], ALU.max).then_inc(f_ready, 1)
                else:
                    v.tensor_tensor(qn[:, n % 2, :].rearrange("p (h d) -> p h d", d=HD), src, r, ALU.mult
                                    ).then_inc(qn_ready, 1)

            def decay():
                dve.wait_ge(f_log, 2)
                v.scalar_tensor_tensor(out=logf[:, :, :], in0=zf[:, :, :], scalar=0.0, in1=ze[:, :, :],
                                       op0=ALU.min, op1=ALU.subtract).then_inc(logf_ready, 1)
                b = t_filled(dve, ("decay",))
                v.tensor_copy(csum[:, :, :], t_ps[b][:, 0:TILES * HEADS].rearrange("p (t h) -> p t h", h=HEADS)
                              ).then_inc(t_free[b], 1)
                dve.wait_ge(t_free[b], T[(("decay",), 0)][1] + 1)
                link(v.tensor_copy(cpart[:, :, 0, :], csum[:, :, :]))
                link(v.tensor_tensor(crest[:, :, :], csum[:, :, :], cpart[:, :, 0, :], ALU.subtract))
                link(v.tensor_copy(cpart[:, :, 1, :], crest[:, :, :]))
                link(v.tensor_tensor(crest[:, :, :], crest[:, :, :], cpart[:, :, 1, :], ALU.subtract))
                v.tensor_copy(cpart[:, :, 2, :], crest[:, :, :]).then_inc(cpart_ready, 1)

            def decay_turn():
                b = t_filled(dve, ("decay_turn",))
                src = t_ps[b][0:24, 0:SEQ // 2].bitcast(BF16)
                v.tensor_copy(cT[:, :], src).then_inc(ct_ready, 1)
                v.tensor_scalar(ncT[:, :], src, -1.0, None, ALU.mult).then_inc(t_free[b], 1)

            def score(g):
                t, i = divmod(g, 16)
                fox, h, _, _ = head_of(i)
                _, n = keys_of(g)
                dve.wait_ge(score_done, g + 1)
                if g == 0:
                    dve.wait_ge(masks_built, 11)
                if g == HEADS:
                    dve.wait_ge(bias_loaded, 16 * HEADS)
                if g >= 2:
                    dve.wait_ge(probs_ready, g - 1)
                if i == 0 and t >= 2:
                    dve.wait_ge(sink_exp, t - 1)
                add = causal[:, SEQ - n * P:SEQ] if fox else swa_bias[:, h, BAND - n * P:BAND]
                v.tensor_tensor_reduce(out=s_sb[:, g % 2, 0:n * P], in0=s_ps[g % 2][:, 0:n * P], in1=add, scale=-1.0,
                                       scalar=-NEG if fox else nsink[:, h:h + 1], op0=ALU.add, op1=ALU.min,
                                       accum_out=negm[:, t % 2, i:i + 1]).then_inc(score_ready, 1)

            def probs(g):
                if g % 2:
                    return
                _, n = keys_of(g)
                b = t_filled(dve, ("probs", g))
                if g >= 2:
                    dve.wait_ge(value_done, g - 1)
                v.tensor_copy(pT[:, g % 2, 0:n * P], t_ps[b][:, 0:n * P]).then_inc(t_free[b], 1)

            def value(g):
                t, i = divmod(g, 16)
                if i == 13:
                    dve.wait_ge(score_ready, 16 * t + 16)
                    if t:
                        dve.wait_ge(sink_exp, t)
                    v.tensor_tensor(sk[:, 0, :], sink_b[:, :], negm[:, t % 2, HEADS:], ALU.add).then_inc(sink_in, 1)
                if i == HEADS - 1 or i == 2 * HEADS - 1:
                    fox = i < HEADS
                    lo = 0 if fox else HEADS
                    dve.wait_ge(value_done, g + 1)
                    dve.wait_ge(probs_ready, g + 1)
                    d = den[:, t % 2, lo:lo + HEADS]
                    if not fox:
                        dve.wait_ge(sink_exp, t + 1)
                        link(v.tensor_tensor(d, d, sk[:, 1, :], ALU.add))
                    link(v.reciprocal(rden[:, lo:lo + HEADS], d))
                    if t:
                        t_filled(dve, ("mix", t - 1), 1)
                    elif fox:
                        t_filled(dve, ("turn", "qb", TILES - 1))
                    v.tensor_tensor(o_sb[:, lo * HD:(lo + HEADS) * HD].rearrange("p (h d) -> p h d", d=HD),
                                    o_ps[0 if fox else 1][:, :].rearrange("p (h d) -> p h d", d=HD),
                                    rden[:, lo:lo + HEADS].unsqueeze(2).broadcast_to([P, HEADS, HD]),
                                    ALU.mult).then_inc(mix_ready, 1)

            def mix(t):
                b = t_filled(dve, ("mix", t), 0)
                v.tensor_copy(mixT[:, 0:4, :], t_ps[b][:, :].rearrange("p (m n) -> p m n", m=4)).then_inc(t_free[b], 1)

            def residual(n, t):
                b, k = A[((f"out{n}", t), 0)]
                dve.wait_ge(a_full[b], k + 1)
                dve.wait_ge(h_in, 16 * (t + 1))
                half = hb[:, n * HALF:(n + 1) * HALF]
                v.tensor_tensor(half, acc_ps[b][:, :], half, ALU.add).then_inc(h_ready, 1)
                if n == 1:
                    if t == 0:
                        dve.wait_ge(tail_loaded, 16)
                        link(v.tensor_scalar(gmoe[:, :], gmoe[:, :], D ** 0.5, None, ALU.mult))
                    dve.wait_ge(rs_ready, TILES * (2 + len(NORMED)) - (TILES - 1 - t))
                    link(v.reciprocal(ss2[:, 1:2], ss2[:, 1:2]))
                    v.scalar_tensor_tensor(out=hn2[:, :], in0=hb[:, :], scalar=ss2[:, 1:2], in1=gmoe[:, :],
                                           op0=ALU.mult, op1=ALU.mult).then_inc(hn2_ready, 1)

            def hn2_(t):
                b = t_filled(dve, ("hn2", t), 0)
                v.tensor_copy(hn2T[:, 0:4, :], t_ps[b][:, :].rearrange("p (m n) -> p m n", m=4)).then_inc(t_free[b], 1)

            def route(t):
                b = t_filled(dve, ("route", t))
                v.tensor_tensor(lg[:, :], t_ps[b][:, 0:EXPERTS], br_b[:, :], ALU.add).then_inc(t_free[b], 1)
                dve.wait_ge(t_free[b], T[(("route", t), 0)][1] + 1)
                link(v.max(top[:, :], lg[:, :]))
                v.tensor_scalar(ntop[:, :], top[:, 0:1], -1.0, None, ALU.mult).then_inc(ntop_ready, 1)
                link(v.max_index(topi[:, :], top[:, :], lg[:, :]))
                link(v.tensor_copy(topf[:, :], topi[:, 0:TOPK]))
                link(v.tensor_tensor(eq[:, :, :], iota_exp[:, :].unsqueeze(1).broadcast_to([P, TOPK, EXPERTS]),
                                     topf[:, :].unsqueeze(2).broadcast_to([P, TOPK, EXPERTS]), ALU.is_equal))
                link(v.tensor_reduce(mask[:, t, :], eq[:, :, :].rearrange("p k e -> p e k"), AX.X, ALU.add))
                v.tensor_copy(mask_b[:, t, :], mask[:, t, :]).then_inc(mask_ready, 1)
                dve.wait_ge(ex_ready, t + 1)
                link(v.reciprocal(exs[:, 1:2], exs[:, 0:1]))
                link(v.tensor_scalar(ex[:, :], ex[:, :], exs[:, 1:2], None, ALU.mult))
                link(v.tensor_tensor(eqg[:, :, :], eq[:, :, :], ex[:, :].unsqueeze(2).broadcast_to([P, TOPK, EXPERTS]),
                                     ALU.mult))
                link(v.tensor_reduce(gsum[:, :], eqg[:, :, :].rearrange("p k e -> p e k"), AX.X, ALU.add))
                link(v.tensor_copy(gate_parts[:, t, :, 0], gsum[:, :]))
                link(v.tensor_tensor(gsum[:, :], gsum[:, :], gate_parts[:, t, :, 0], ALU.subtract))
                link(v.tensor_copy(gate_parts[:, t, :, 1], gsum[:, :]))
                link(v.tensor_tensor(gsum[:, :], gsum[:, :], gate_parts[:, t, :, 1], ALU.subtract))
                link(v.tensor_copy(gate_parts[:, t, :, 2], gsum[:, :]))

            def place():
                b = t_filled(dve, ("place",))
                link(v.scalar_tensor_tensor(
                    out=posm[:, :, :], in0=t_ps[b][:, 0:TILES * EXPERTS].rearrange("p (t e) -> p t e", e=EXPERTS),
                    scalar=1.0, in1=mask[:, :, :], op0=ALU.add, op1=ALU.mult))
                link(v.tensor_scalar(posm[:, :, :], posm[:, :, :], -1.0, None, ALU.add))
                dve.wait_ge(rows_stored, 16 * (2 * TILES + 1))
                dve.wait_ge(ex_ready, TILES)
                v.tensor_copy(ocnt[:, :], t_ps[b][0:EXPERTS, 128:129]).then_inc(placed, 1)

            does = {"hn": hn, "toep": toep, "proj": proj, "decay": decay, "decay_turn": decay_turn,
                    "score": score, "probs": probs, "value": value, "mix": mix,
                    "out0": lambda t: residual(0, t), "out1": lambda t: residual(1, t),
                    "hn2": hn2_, "route": route, "place": place}
            for s in order:
                if s[0] in does:
                    does[s[0]](*s[1:])

            def indices(s):
                dve.wait_ge(idx_psum, s + 1)
                if later(s):
                    dve.wait_ge(cur_ready, s * 2)
                v.tensor_reduce(tokf[:, :], gate_ps[0][:, 0:2], AX.X, ALU.add).then_inc(idx_sum, 1)
                v.tensor_reduce(gate_next[:, :], gate_ps[0][:, 2:5], AX.X, ALU.add).then_inc(idx_sum, 1)
                dve.wait_ge(idx_sum, s * 2 + 2)
                if later(s):
                    dve.wait_ge(gathered, s * 16)
                v.tensor_scalar(sidx_next[:, :], tokf[:, :], 1024.0, slot_trash[:, 0:1], ALU.add, ALU.min
                                ).then_inc(idx_ready, 1)
                v.tensor_scalar(gidx[:, :], tokf[:, :], 1024.0, None, ALU.add).then_inc(idx_ready, 1)

            def current(t):
                dve.wait_ge(idx_ready, t * 2 + 2)
                if later(t):
                    dve.wait_ge(y_ready, t)
                    dve.wait_ge(scattered, t * 16)
                v.tensor_copy(gate[:, :], gate_next[:, :]).then_inc(cur_ready, 1)
                v.tensor_copy(sidx[:, :], sidx_next[:, :]).then_inc(cur_ready, 1)

            def swiglu_gate(t):
                dve.wait_ge(gate_psum, t + 1)
                if later(t):
                    dve.wait_ge(sig_ready, t)
                for half in range(2):
                    c = slice(half * HALF, (half + 1) * HALF)
                    last = v.tensor_scalar(gmin[:, c], gate_ps[half][:, :], LIMIT, None, ALU.min)
                last.then_inc(gmin_ready, 1)

            def swiglu_rest(t):
                dve.wait_ge(sig_ready, t + 1)
                dve.wait_ge(gmin_ready, t + 1)
                v.tensor_tensor(gs[:, :], gmin[:, :], sig[:, :], ALU.mult).then_inc(gs_ready, 1)
                dve.wait_ge(up_psum, t + 1)
                for half in range(2):
                    c = slice(half * HALF, (half + 1) * HALF)
                    v.tensor_scalar(up[:, c], up_ps[half][:, :], LIMIT, -LIMIT, ALU.min, ALU.max).then_inc(up_ready, 1)
                dve.wait_ge(gs_ready, t + 1)
                for half in range(2):
                    c = slice(half * HALF, (half + 1) * HALF)
                    dve.wait_ge(up_ready, t * 2 + half + 1)
                    if later(t) and half == 0:
                        dve.wait_ge(act_transposed, t * 2)
                    v.scalar_tensor_tensor(out=act_sb[:, c], in0=up[:, c], scalar=1.0, in1=gs[:, c],
                                           op0=ALU.add, op1=ALU.mult).then_inc(act_ready, 1)
                dve.wait_ge(act_transposed, t * 2 + 2)
                v.tensor_copy(actT[:, 4:8, :], turn_ps[1][:, :].rearrange("p (m n) -> p m n", m=4)
                              ).then_inc(actT1_ready, 1)

            def expert(t, ahead):
                current(t)
                swiglu_gate(t)
                if ahead:
                    indices(t + 1)
                swiglu_rest(t)

            indices(0)
            dve.wait_ge(bias_raw, 16 * 6)
            link(v.tensor_copy(bias_tab[:, :], btmp[:, :]))
            for part in range(1, 3):
                for r in range(part, 3):
                    rows = slice(32 * r, 32 * r + 32)
                    link(v.tensor_tensor(btmp[rows, :], btmp[rows, :], bias_tab[rows, :], ALU.subtract))
                    last = v.tensor_copy(bias_tab[rows, :], btmp[rows, :])
                    if (part, r) == (2, 2):
                        last.then_inc(bias_ready, 1)
                    else:
                        link(last)
            dve.wait_ge(placed, 1)
            link(v.tensor_scalar(oext[:, :], ocnt[:, :], float(P), None, ALU.is_gt))
            for r in (2, 3):
                link(v.scalar_tensor_tensor(out=oext[:, :], in0=ocnt[:, :], scalar=float(r * P), in1=oext[:, :],
                                            op0=ALU.is_gt, op1=ALU.add))
            v.tensor_copy(oext_b[:, :], oext[:, :]).then_inc(over_step, 1)
            dve.wait_ge(over_pe, 1)
            link(v.tensor_copy(ostart[:, :], turn_ps[0][0:32, 0:1]))
            link(v.tensor_scalar(odif[:, :], iota_slot[0:32, 0:16], ostart[:, 0:1], None, ALU.subtract))
            link(v.tensor_scalar(ooh[:, 0, :], odif[:, :], 0.0, None, ALU.is_ge))
            link(v.scalar_tensor_tensor(out=ooh[:, 2, :], in0=odif[:, :], scalar=oext[:, 0:1], in1=ooh[:, 0, :],
                                        op0=ALU.is_lt, op1=ALU.mult))
            link(v.scalar_tensor_tensor(out=ooh[:, 1, :], in0=odif[:, :], scalar=1.0, in1=ooh[:, 2, :],
                                        op0=ALU.add, op1=ALU.mult))
            v.tensor_scalar(ooh[:, 0, :], ooh[:, 2, :], lane[0:32, 0:1], None, ALU.mult).then_inc(over_step, 1)
            dve.wait_ge(over_pe, 2)
            v.tensor_copy(over_tab[:, :], turn_ps[1][0:1, 0:48]).then_inc(over_ready, 1)

            expert(0, True)
            with dve.Fori(1, EXPERTS - 1) as t:
                expert(t, True)
            expert(EXPERTS - 1, False)
            dve.wait_ge(over_ready, 1)
            with dve.Fori(0, OVER) as j:
                used = dve.value_load(over_tab[0:1, bass.ds(j + 32, 1)], min_val=0, max_val=1)
                with dve.If(used > 0):
                    indices(j + EXPERTS)
                    expert(j + EXPERTS, False)

        @block.tensor
        def _(pe):
            def t_claim(key, half=0):
                b, n = T[(key, half)]
                if n:
                    pe.wait_ge(t_free[b], n)
                return b

            held = {}

            def a_claim(key):
                b, n = A[(key, 0)]
                if n:
                    last = held[b]
                    t = last[-1]
                    if last[0] != "proj":
                        pe.wait_ge(h_ready, 2 * t + int(last[0][-1]) + 1)
                    elif last[1] == "va":
                        pe.wait_ge(va_ready, t + 1)
                    elif last[1] == "kvf":
                        pe.wait_ge(vb_ready, t + 1)
                        pe.wait_ge(zf_ready, t + 1)
                    else:
                        pe.wait_ge(qn_ready, NORMED.index(last[1]) * TILES + t + 1 + TILES)
                held[b] = key
                return b

            def hn(t):
                pe.wait_ge(xn_ready, t + 1)
                if t == 0:
                    pe.wait_ge(masks_built, 11)
                for half in range(2):
                    b = t_claim(("hn", t), half)
                    for m in range(4):
                        k = 4 * half + m
                        last = pe.transpose(t_ps[b][:, m * P:(m + 1) * P], xt[:, t % 2, k * P:(k + 1) * P], ident[:, :])
                    last.then_inc(t_full[b], 1)

            def toep(h):
                if h == 0:
                    pe.wait_ge(lams_ready, 1)
                b = t_claim(("toep", h))
                pe.matmul(t_ps[b][:, 0:TOEP], lams[:, h, :], tabs, start=True, stop=True).then_inc(t_full[b], 1)

            def proj(c, t):
                n = CH.index(c)
                if t == 0:
                    loads = [32, 16, 48, 32, 64]
                    pe.wait_ge(win_loaded[n % 2], loads[n])
                    if n == 0:
                        for u in range(TILES):
                            for half in range(2):
                                t_evacuated(pe, ("hn", u), half)
                w = HW if c != "kvf" else KVF
                b = a_claim(("proj", c, t))
                for k in range(KT):
                    last = pe.matmul(acc_ps[b][:, 0:w], hnT[:, k, t * P:(t + 1) * P], w_buf[n % 2][:, k, 0:w],
                                     start=(k == 0), stop=(k == KT - 1))
                last.then_inc(a_full[b], 1)

            def turn(c, t):
                n = NORMED.index(c) * TILES + t
                pe.wait_ge(qn_ready, 2 * (n + 1) if c == "kvf" else n + 1 + TILES)
                b = t_claim(("turn", c, t))
                m_ = 2 if c == "kvf" else 4
                for m in range(m_):
                    last = pe.transpose(t_ps[b][:, m * P:(m + 1) * P], qn[:, n % 2, m * P:(m + 1) * P], ident[:, :])
                last.then_inc(t_full[b], 1)

            def decay():
                pe.wait_ge(logf_ready, 1)
                b = t_claim(("decay",))
                for t in range(TILES):
                    dst = t_ps[b][:, t * HEADS:(t + 1) * HEADS]
                    for s in range(t):
                        pe.matmul(dst, ones[:, :], logf[:, s, :], start=(s == 0), stop=False)
                    last = pe.matmul(dst, tri[:, :], logf[:, t, :], start=(t == 0), stop=True)
                last.then_inc(t_full[b], 1)

            def decay_turn():
                pe.wait_ge(cpart_ready, 1)
                b = t_claim(("decay_turn",))
                dst = t_ps[b][0:24, 0:SEQ // 2].bitcast(BF16)
                for t in range(TILES):
                    last = pe.transpose(dst[:, t * P:(t + 1) * P], cpart[:, t, :, :].rearrange("p a h -> p (a h)"),
                                        ident_b[:, :])
                last.then_inc(t_full[b], 1)

            def score(g):
                t, i = divmod(g, 16)
                fox, h, pair, base = head_of(i)
                first, n = keys_of(g)
                if g == 0:
                    for s in (("turn", "ka", TILES - 1), ("turn", "qa", TILES - 1), ("decay_turn",)):
                        t_evacuated(pe, s)
                    for u in range(TILES):
                        t_evacuated(pe, ("turn", "qa", u))
                    pe.wait_ge(ct_ready, 1)
                if g == HEADS:
                    for u in range(TILES):
                        t_evacuated(pe, ("turn", "qb", u))
                if g >= 2:
                    pe.wait_ge(score_ready, g - 1)
                dst = s_ps[g % 2][:, 0:n * P]
                q = (qaT if fox else qbT)[base:base + HD, pair, t * P:(t + 1) * P]
                k = (kaT[base:base + HD, pair, 0:n * P] if fox
                     else kbT[base:base + HD, h // GROUP, first * P:(first + n) * P])
                last = pe.matmul(dst, q, k, start=True, stop=not fox)
                if fox:
                    pe.matmul(dst, head_row[:, h, :], ncT[:, 0:n * P], start=False, stop=False)
                    last = pe.matmul(dst, cT[:, t * P:(t + 1) * P],
                                     head_row[:, h, :].unsqueeze(1).broadcast_to([24, n, P]),
                                     start=False, stop=True)
                last.then_inc(score_done, 1)

            def probs(g):
                _, n = keys_of(g)
                pe.wait_ge(probs_ready, g + 1)
                b = t_claim(("probs", g))
                for m in range(n):
                    last = pe.transpose(t_ps[b][:, m * P:(m + 1) * P], p_sb[:, g % 2, m * P:(m + 1) * P], ident[:, :])
                last.then_inc(t_full[b], 1)

            def value(g):
                t, i = divmod(g, 16)
                fox, h, _, _ = head_of(i)
                first, n = keys_of(g)
                t_evacuated(pe, ("probs", g))
                if g == 0:
                    pe.wait_ge(va_ready, TILES)
                if g == HEADS:
                    pe.wait_ge(vb_ready, TILES)
                if t and h == 0:
                    pe.wait_ge(mix_ready, 2 * t - (1 if fox else 0))
                dst = o_ps[0 if fox else 1][:, h * HD:(h + 1) * HD]
                for m in range(n):
                    val = va[:, first + m, h * HD:(h + 1) * HD] if fox else \
                        vb[:, first + m, (h // GROUP) * HD:(h // GROUP + 1) * HD]
                    last = pe.matmul(dst, pT[:, g % 2, m * P:(m + 1) * P], val, start=(m == 0), stop=(m == n - 1))
                last.then_inc(value_done, 1)

            def mix(t):
                pe.wait_ge(mix_ready, 2 * t + 2)
                for half in range(2):
                    b = t_claim(("mix", t), half)
                    for m in range(4):
                        k = 4 * half + m
                        last = pe.transpose(t_ps[b][:, m * P:(m + 1) * P], o_sb[:, k * P:(k + 1) * P], ident[:, :])
                    last.then_inc(t_full[b], 1)

            def outp(n, t):
                if n == 0:
                    t_evacuated(pe, ("mix", t), 0)
                    t_evacuated(pe, ("mix", t), 1)
                    if t == 0:
                        pe.wait_ge(wout_loaded, 16)
                b = a_claim((f"out{n}", t))
                for k in range(KT):
                    last = pe.matmul(acc_ps[b][:, :], mixT[:, k, :], wout_sb[:, k, n * HALF:(n + 1) * HALF],
                                     start=(k == 0), stop=(k == KT - 1))
                last.then_inc(a_full[b], 1)

            def hn2_(t):
                pe.wait_ge(hn2_ready, t + 1)
                for half in range(2):
                    b = t_claim(("hn2", t), half)
                    for m in range(4):
                        k = 4 * half + m
                        last = pe.transpose(t_ps[b][:, m * P:(m + 1) * P], hn2[:, k * P:(k + 1) * P], ident[:, :])
                    last.then_inc(t_full[b], 1)

            def route(t):
                t_evacuated(pe, ("hn2", t), 0)
                t_evacuated(pe, ("hn2", t), 1)
                b = t_claim(("route", t))
                for k in range(KT):
                    last = pe.matmul(t_ps[b][:, 0:EXPERTS], hn2T[:, k, :], wr[:, k, :], start=(k == 0),
                                     stop=(k == KT - 1))
                last.then_inc(t_full[b], 1)

            def place():
                pe.wait_ge(mask_ready, TILES)
                b = t_claim(("place",))
                for t in range(TILES):
                    dst = t_ps[b][:, t * EXPERTS:(t + 1) * EXPERTS]
                    for s in range(t):
                        pe.matmul(dst, ones_b[:, :], mask_b[:, s, :], start=(s == 0), stop=False)
                    pe.matmul(dst, before[:, :], mask_b[:, t, :], start=(t == 0), stop=True)
                for s in range(TILES):
                    last = pe.matmul(t_ps[b][0:EXPERTS, 128:129], mask_b[:, s, :], ones_b[:, 0:1], start=(s == 0),
                                     stop=(s == TILES - 1))
                last.then_inc(t_full[b], 1)

            does = {"hn": hn, "toep": toep, "proj": proj, "turn": turn, "decay": decay, "decay_turn": decay_turn,
                    "score": score, "probs": probs, "value": value, "mix": mix,
                    "out0": lambda t: outp(0, t), "out1": lambda t: outp(1, t), "hn2": hn2_, "route": route,
                    "place": place}
            for s in order:
                if s[0] in does:
                    does[s[0]](*s[1:])

            def chunk(c):
                return ring[:, c * CHUNK_COLS:(c + 1) * CHUNK_COLS].rearrange("p (k n) -> p k n", k=2)

            def indices(s):
                pe.wait_ge(onehot_ready, s * TILES + TILES)
                for j in range(TILES):
                    last = pe.matmul(gate_ps[0][:, 0:5], slot_oh[:, j, :], idx_rhs[:, j, :], start=(j == 0),
                                     stop=(j == TILES - 1))
                last.then_inc(idx_psum, 1)

            def turn_rows(s, results):
                pe.wait_ge(gathered, s * 16 + 16)
                if later(results):
                    pe.wait_ge(y_ready, results)
                for k in range(KT):
                    last = pe.transpose(y_ps[k // 4][:, (k % 4) * P:(k % 4 + 1) * P], gx[:, k * P:(k + 1) * P],
                                        ident[:, :])
                last.then_inc(x_transposed, 1)

            def products(t, dst, stat, chunks, start):
                for c in chunks:
                    pe.wait_ge(w_loaded[c], t * 16 + 16)
                    for k in range(2):
                        kt = 2 * (c % 4) + k
                        for n in range(2):
                            last = pe.matmul(dst[n][:, :], stat[:, kt, :], chunk(c)[:, k, n * HALF:(n + 1) * HALF],
                                             start=(start and kt == 0), stop=False)
                    if c % 4 != 3:
                        last.then_inc(chunk_used, 1)
                    else:
                        last.then_inc(chunk_used, 1)

            def biases(dst, col, done):
                for n in range(2):
                    last = pe.matmul(dst[n][:, :], bias_sel[:, :], bias_tab[:, col + n * HALF:col + (n + 1) * HALF],
                                     start=False, stop=True)
                last.then_inc(done, 1)

            def expert(t, ahead):
                pe.wait_ge(xT_ready, t * 2 + 2)
                pe.wait_ge(idx_ready, t * 2 + 2)
                if later(t):
                    pe.wait_ge(gmin_ready, t)
                products(t, gate_ps, xT, range(0, 4), True)
                pe.wait_ge(sel_ready, t + 1)
                biases(gate_ps, 0, gate_psum)
                if later(t):
                    pe.wait_ge(up_ready, t * 2)
                products(t, up_ps, xT, range(4, 6), True)
                if ahead:
                    pe.wait_ge(gmin_ready, t + 1)
                    indices(t + 1)
                products(t, up_ps, xT, range(6, 8), False)
                biases(up_ps, D, up_psum)
                if ahead:
                    turn_rows(t + 1, t)
                for half in range(2):
                    pe.wait_ge(act_ready, t * 2 + half + 1)
                    if later(t):
                        pe.wait_ge(actT1_ready if half else actT0_ready, t)
                    for m in range(4):
                        k = 4 * half + m
                        last = pe.transpose(turn_ps[half][:, m * P:(m + 1) * P], act_sb[:, k * P:(k + 1) * P],
                                            ident[:, :])
                    last.then_inc(act_transposed, 1)
                if ahead:
                    pe.wait_ge(xT_ready, t * 2 + 4)
                elif later(t):
                    pe.wait_ge(y_ready, t)
                pe.wait_ge(actT0_ready, t + 1)
                products(t, y_ps, actT, range(8, 10), True)
                pe.wait_ge(actT1_ready, t + 1)
                products(t, y_ps, actT, range(10, 12), False)
                biases(y_ps, 2 * D, y_psum)

            pe.wait_ge(placed, 1)
            indices(0)
            pe.wait_ge(over_step, 1)
            pe.matmul(turn_ps[0][0:32, 0:1], before[0:32, 0:32], oext_b[:, :], start=True, stop=True
                      ).then_inc(over_pe, 1)
            pe.wait_ge(over_step, 2)
            pe.matmul(turn_ps[1][:, 0:48], ones_f[:, :], ooh[:, :, :].rearrange("p a j -> p (a j)"),
                      start=True, stop=True).then_inc(over_pe, 1)
            turn_rows(0, 0)
            pe.wait_ge(bias_ready, 1)
            pe.wait_ge(over_ready, 1)
            expert(0, True)
            with pe.Fori(1, EXPERTS - 1) as t:
                expert(t, True)
            expert(EXPERTS - 1, False)
            with pe.Fori(0, OVER) as j:
                used = pe.value_load(over_tab[0:1, bass.ds(j + 32, 1)], min_val=0, max_val=1)
                with pe.If(used > 0):
                    indices(j + EXPERTS)
                    turn_rows(j + EXPERTS, j + EXPERTS)
                    expert(j + EXPERTS, False)


_INS = ["x", "norm_mix", "w_in", "b_forget", "q_norm_fox", "k_norm_fox", "q_norm_swa", "k_norm_swa", "sinks",
        "rel_bias", "w_out", "norm_moe", "w_router", "b_router", "w_up_gate", "b_up_gate", "w_down", "b_down"]


def kernel(**inputs):
    import numpy as _np
    import concourse.bacc as _bacc
    from concourse import mybir as _mybir
    from concourse.bass_utils import run_bass_kernel_spmd as _run

    nc = _bacc.Bacc("TRN2", target_bir_lowering=False, num_devices=1)
    arrays, args = {}, []
    for name in _INS:
        a = _np.ascontiguousarray(inputs[name])
        arrays[f"in_{name}_dram"] = a
        args.append(nc.dram_tensor(f"in_{name}_dram", a.shape, _mybir.dt.from_np(a.dtype), kind="ExternalInput").ap())
    table = bucket_table()
    arrays["in_buckets_dram"] = table
    args.append(nc.dram_tensor("in_buckets_dram", table.shape, _mybir.dt.float32, kind="ExternalInput").ap())
    args.append(nc.dram_tensor("out_0_dram", (OUT_ROWS, D), _mybir.dt.float32, kind="ExternalOutput").ap())
    layer_kernel(nc, *args)
    r = _run(nc, [arrays], core_ids=[0])
    return r.results[0]["out_0_dram"][:SEQ].reshape(1, SEQ, D)
```

```python
from contextlib import ExitStack

import numpy as np

import concourse.bass as bass
from concourse import mybir

F32 = mybir.dt.float32
BF16 = mybir.dt.bfloat16
U32 = mybir.dt.uint32
I32 = mybir.dt.int32
ALU = mybir.AluOpType
ACT = mybir.ActivationFunctionType
AX = mybir.AxisListType

P = 128
SEQ = 512
D = 1024
TILES = SEQ // P
KT = D // P
HD = 64
HEADS = 8
KV = 2
GROUP = HEADS // KV
BUCKETS = 32
WINDOW = 128
MAX_DISTANCE = 128
EXPERTS = 32
TOPK = 4
LIMIT = 7.0
ALPHA = 1.702
EPS = 1e-6
NEG = -1e30
BAND = 2 * WINDOW
TOEP = 3 * WINDOW
HALF = 512
HW = HEADS * HD
IN_WIDTH = 4 * HW + HEADS + 2 * KV * HD
OUT_ROWS = SEQ + P
OVER = TOPK * SEQ // P - 1
CHUNKS = 12
CHUNK_COLS = 2 * D

QA, KA, VA, FG, QB, KB = 0, HW, 2 * HW, 3 * HW, 3 * HW + HEADS, 4 * HW + HEADS
CH = ["kvf", "ka", "va", "qa", "qb"]
CH_AT = {"ka": KA, "va": VA, "qa": QA, "qb": QB}
KVF = 2 * KV * HD + HEADS
NORMED = ["kvf", "ka", "qa", "qb"]


def later(t):
    return not (isinstance(t, int) and t == 0)


def bucket_table():
    table = np.zeros((BUCKETS + 1, TOEP), np.float32)
    for m in range(TOEP):
        n = 2 * WINDOW - 1 - m
        if not 0 <= n < WINDOW:
            table[BUCKETS, m] = NEG
            continue
        half = BUCKETS // 2
        if n < half:
            b = n
        else:
            large = np.log(np.float32(n) / np.float32(half)) / np.float32(np.log(MAX_DISTANCE / half))
            b = min(half + int(np.float32(large) * np.float32(BUCKETS - half)), BUCKETS - 1)
        table[b, m] = 1.0
    return table


def schedule():
    order = [("toep", 0), ("toep", 1), ("toep", 2), ("xn", 0), ("toep", 3), ("hn", 0), ("xn", 1), ("toep", 4),
             ("hn", 1), ("toep", 5), ("xn", 2), ("toep", 6), ("hn", 2), ("xn", 3), ("toep", 7), ("hn", 3)]
    units = [(c, t) for c in CH for t in range(TILES)]
    for n, (c, t) in enumerate(units):
        order.append(("proj", c, t))
        if n >= 2 and units[n - 2][0] in NORMED:
            order.append(("turn", *units[n - 2]))
        if n == 6:
            order.append(("forget",))
        if n == 9:
            order.append(("decay",))
        if n == 11:
            order.append(("decay_turn",))
    order += [("score", 0), ("turn", *units[-2]), ("score", 1), ("turn", *units[-1])]
    total = TILES * 2 * HEADS
    fill = {3: "mix", 5: "out0", 6: "squares0", 7: "out1", 8: "squares1", 10: "norm2", 12: "hn2"}
    for g in range(total):
        order.append(("probs", g))
        if g + 2 < total:
            order.append(("score", g + 2))
        if g:
            order.append(("value", g - 1))
        t, i = divmod(g, 2 * HEADS)
        if i == HEADS + 1:
            order.append(("norm", t, 0))
        if t and i == 1:
            order.append(("norm", t - 1, 1))
        if t and i in fill:
            order.append((fill[i], t - 1))
        if t >= 2 and i == 5:
            order.append(("route", t - 2))
        if t >= 2 and i == 6:
            order.append(("gates", t - 2))
    order += [("value", total - 1), ("norm", TILES - 1, 1)]
    last = TILES - 1
    order += [("mix", last), ("out0", last), ("route", last - 1), ("gates", last - 1),
              ("squares0", last), ("out1", last), ("squares1", last), ("norm2", last), ("hn2", last), ("route", last)]
    order += [("place",), ("tokens",), ("gates", TILES - 1)]
    return order


def bank_plan(order):
    turns, accs = [], []
    for s in order:
        if s[0] in ("hn", "mix", "hn2"):
            turns += [(s, 0), (s, 1)]
        elif s[0] in ("toep", "turn", "decay", "decay_turn", "probs", "route", "place"):
            turns.append((s, 0))
        elif s[0] in ("proj", "out0", "out1"):
            accs.append((s, 0))
    return {k: (n % 2, n // 2) for n, k in enumerate(turns)}, {k: (n % 2, n // 2) for n, k in enumerate(accs)}


def layer_kernel(nc, x, norm_mix, w_in, b_forget, q_norm_fox, k_norm_fox, q_norm_swa, k_norm_swa, sinks,
                 rel_bias, w_out, norm_moe, w_router, b_router, w_up_gate, b_up_gate, w_down, b_down,
                 buckets, out):
    order = schedule()
    T, A = bank_plan(order)

    toep_dram = nc.dram_tensor("toeplitz_rows", [P, HEADS * TOEP], F32, kind="Internal").ap()
    hn2_dram = nc.dram_tensor("normed_rows", [SEQ, D], F32, kind="Internal").ap()

    ctx = ExitStack()
    with ctx:
        def sb(name, shape, dt=F32, at=ctx):
            return at.enter_context(nc.sbuf_tensor(name, shape, dt))

        def sem(name):
            return ctx.enter_context(nc.semaphore(name))

        ring = sb("ring", [P, CHUNKS * CHUNK_COLS])
        ident = sb("ident", [P, P])
        ident_b = sb("ident_b", [P, P], BF16)
        ones_b = sb("ones_b", [P, P], BF16)
        before = sb("before", [P, P], BF16)
        iota_slot = sb("iota_slot", [P, SEQ])
        iota_exp = sb("iota_exp", [P, EXPERTS])
        lane = sb("lane", [P, 1])
        slot_trash = sb("slot_trash", [P, 1])
        gate_parts = sb("gate_parts", [P, TILES, EXPERTS, 3], BF16)
        posm = sb("posm", [P, TILES, EXPERTS])
        bias_tab = sb("bias_tab", [96, 3 * D], BF16)
        expert_row = sb("expert_row", [96, EXPERTS], BF16)
        iota_blk = sb("iota_blk", [P, P])
        idx_rhs = sb("idx_rhs", [P, TILES, 5], BF16)
        ones_f = sb("ones_f", [32, P])
        poscol = sb("poscol", [P, TILES])
        slot_oh = sb("slot_oh", [P, TILES, P], BF16)
        over_tab = sb("over_tab", [1, 3 * 16], I32)

        early = ExitStack()
        qaT = sb("qaT", [P, 4, SEQ], at=early)
        kaT = sb("kaT", [P, 4, SEQ], at=early)
        qbT = sb("qbT", [P, 4, SEQ], at=early)
        kbT = sb("kbT", [P, KV, SEQ], at=early)
        va = sb("va", [P, TILES, HW], at=early)
        vb = sb("vb", [P, TILES, KV * HD], at=early)
        swa_bias = sb("swa_bias", [P, HEADS, BAND], at=early)
        causal = sb("causal", [P, SEQ], at=early)
        s_sb = sb("s_sb", [P, 2, HALF], at=early)
        p_sb = sb("p_sb", [P, 2, HALF], at=early)
        pT = sb("pT", [P, 2, HALF], at=early)
        cT = sb("cT", [24, SEQ], BF16, at=early)
        ncT = sb("ncT", [24, SEQ], BF16, at=early)
        head_row = sb("head_row", [24, HEADS, P], BF16, at=early)
        gcols = sb("gcols", [P, 4], at=early)
        gmix = sb("gmix", [P, KT], at=early)
        bf_b = sb("bf_b", [P, HEADS], at=early)
        sink_b = sb("sink_b", [P, HEADS], at=early)
        nsink = sb("nsink", [P, HEADS], at=early)
        br_b = sb("br_b", [P, EXPERTS], at=early)
        wr = sb("wr", [P, KT, EXPERTS], at=early)
        rel = sb("rel", [BUCKETS + 1, HEADS], at=early)
        ss = sb("ss", [P, 8], at=early)
        rs = sb("rs", [P, 8], at=early)
        eps_d = sb("eps_d", [P, 1], at=early)
        eps_h = sb("eps_h", [P, 1], at=early)
        ssx = sb("ssx", [P, TILES], at=early)
        rsx = sb("rsx", [P, TILES], at=early)
        zf = sb("zf", [P, TILES, HEADS], at=early)
        za = sb("za", [P, TILES, HEADS], at=early)
        ze = sb("ze", [P, TILES, HEADS], at=early)
        logf = sb("logf", [P, TILES, HEADS], at=early)
        tri = sb("tri", [P, P], at=early)
        ones = sb("ones", [P, P], at=early)
        csum = sb("csum", [P, TILES, HEADS], at=early)
        crest = sb("crest", [P, TILES, HEADS], at=early)
        cpart = sb("cpart", [P, TILES, 3, HEADS], BF16, at=early)
        negm = sb("negm", [P, 2, 2 * HEADS], at=early)
        den = sb("den", [P, 2, 2 * HEADS], at=early)
        sk = sb("sk", [P, 2, HEADS], at=early)
        rden = sb("rden", [P, 2 * HEADS], at=early)
        lg = sb("lg", [P, EXPERTS], at=early)
        top = sb("top", [P, 8], at=early)
        topi = sb("topi", [P, 8], U32, at=early)
        topf = sb("topf", [P, TOPK], at=early)
        ntop = sb("ntop", [P, 1], at=early)
        ex = sb("ex", [P, TOPK], at=early)
        exs = sb("exs", [P, 2], at=early)
        eq = sb("eq", [P, TOPK, EXPERTS], at=early)
        eqg = sb("eqg", [P, TOPK, EXPERTS], at=early)
        gsum = sb("gsum", [P, EXPERTS], at=early)
        mask = sb("mask", [P, TILES, EXPERTS], at=early)
        mask_b = sb("mask_b", [P, TILES, EXPERTS], BF16, at=early)
        ss2 = sb("ss2", [P, 2], at=early)
        spare = sb("spare", [P, 1], at=early)

        proj_mem = ExitStack()
        hnT = sb("hnT", [P, KT, SEQ], at=proj_mem)
        xt = sb("xt", [P, 2, D], at=proj_mem)
        qn = sb("qn", [P, 2, HW], at=proj_mem)
        sq = pT[:, 1, :]
        proj_mem.close()
        tail_mem = ExitStack()
        o_sb = sb("o_sb", [P, D], at=tail_mem)
        mixT = sb("mixT", [P, KT, P], at=tail_mem)
        hb = sb("hb", [P, D], at=tail_mem)
        hn2 = sb("hn2", [P, D], at=tail_mem)
        hn2T = sb("hn2T", [P, KT, P], at=tail_mem)
        gmoe = sb("gmoe", [P, D], at=tail_mem)
        tail_mem.close()
        early.close()

        late = ExitStack()
        gx = sb("gx", [P, D], at=late)
        xT = sb("xT", [P, KT, P], at=late)
        gmin = sb("gmin", [P, D], at=late)
        sig = sb("sig", [P, D], at=late)
        gs = sb("gs", [P, D], at=late)
        up = sb("up", [P, D], at=late)
        act_sb = sb("act_sb", [P, D], at=late)
        actT = sb("actT", [P, KT, P], at=late)
        y_sb = sb("y_sb", [P, D], at=late)
        bias_sel = sb("bias_sel", [96, P], BF16, at=late)
        tokf = sb("tokf", [P, 1], at=late)
        gidx = sb("gidx", [P, 1], U32, at=late)
        sidx_next = sb("sidx_next", [P, 1], at=late)
        gate_next = sb("gate_next", [P, 1], at=late)
        sidx = sb("sidx", [P, 1], U32, at=late)
        gate = sb("gate", [P, 1], at=late)
        ocnt = sb("ocnt", [32, 1], at=late)
        oext = sb("oext", [32, 1], at=late)
        oext_b = sb("oext_b", [32, 1], BF16, at=late)
        ostart = sb("ostart", [32, 1], at=late)
        odif = sb("odif", [32, 16], at=late)
        ooh = sb("ooh", [32, 3, 16], at=late)
        late.close()

        w_buf = [ring[:, (8 + 2 * b) * CHUNK_COLS:(10 + 2 * b) * CHUNK_COLS].rearrange("p (k n) -> p k n", k=KT)
                 for b in range(2)]
        wout_sb = ring[:, 8 * CHUNK_COLS:12 * CHUNK_COLS].rearrange("p (k n) -> p k n", k=KT)
        toep_sb = ring[:, 6 * CHUNK_COLS:6 * CHUNK_COLS + HEADS * TOEP]
        lams = ring[0:BUCKETS + 1, 4 * CHUNK_COLS:4 * CHUNK_COLS + HEADS * P].rearrange("b (h p) -> b h p", p=P)
        tabs = ring[0:BUCKETS + 1, 5 * CHUNK_COLS:5 * CHUNK_COLS + TOEP]

        bias_rest = ring[0:96, 0:3 * D]

        banks = [ctx.enter_context(nc.psum_tensor(f"bank{i}", [P, HALF], F32)) for i in range(8)]
        acc_ps, s_ps, t_ps, o_ps = banks[0:2], banks[2:4], banks[4:6], banks[6:8]
        gate_ps, up_ps, y_ps, turn_ps = banks[0:2], banks[2:4], banks[6:8], banks[4:6]

        x_loaded = [sem(f"x_loaded{i}") for i in range(2)]
        small_loaded = sem("small_loaded")
        rel_loaded = sem("rel_loaded")
        tail_loaded = sem("tail_loaded")
        win_loaded = [sem(f"win_loaded{i}") for i in range(2)]
        wout_loaded = sem("wout_loaded")
        consts = sem("consts")
        masks_built = sem("masks_built")
        toep_stored = sem("toep_stored")
        bias_loaded = sem("bias_loaded")
        xn_sq = sem("xn_sq")
        xn_ready = sem("xn_ready")
        eps_ready = sem("eps_ready")
        rs_ready = sem("rs_ready")
        gcols_ready = sem("gcols_ready")
        lams_ready = sem("lams_ready")
        ct_ready = sem("ct_ready")
        sink_in = sem("sink_in")
        va_ready = sem("va_ready")
        vb_ready = sem("vb_ready")
        zf_ready = sem("zf_ready")
        t_full = [sem(f"t_full{i}") for i in range(2)]
        t_free = [sem(f"t_free{i}") for i in range(2)]
        a_full = [sem(f"a_full{i}") for i in range(2)]
        sq_ready = sem("sq_ready")
        sq_free = sem("sq_free")
        qn_ready = sem("qn_ready")
        f_ready = sem("f_ready")
        f_log = sem("f_log")
        logf_ready = sem("logf_ready")
        cpart_ready = sem("cpart_ready")
        score_ready = sem("score_ready")
        score_done = sem("score_done")
        probs_ready = sem("probs_ready")
        value_done = sem("value_done")
        sink_exp = sem("sink_exp")
        mix_ready = sem("mix_ready")
        h_in = sem("h_in")
        h_ready = sem("h_ready")
        h_sq = sem("h_sq")
        hn2_ready = sem("hn2_ready")
        rows_stored = sem("rows_stored")
        ntop_ready = sem("ntop_ready")
        ex_ready = sem("ex_ready")
        mask_ready = sem("mask_ready")
        step = sem("step")
        gates_ready = sem("gates_ready")
        placed = sem("placed")
        w_loaded = [sem(f"w_loaded{c}") for c in range(CHUNKS)]
        chunk_used = sem("chunk_used")
        late_consts = sem("late_consts")
        bias_raw = sem("bias_raw")
        bias_split = sem("bias_split")
        over_step = sem("over_step")
        over_pe = sem("over_pe")
        over_ready = sem("over_ready")
        cols_copied = sem("cols_copied")
        onehot_ready = sem("onehot_ready")
        tok_psum = sem("tok_psum")
        idx_psum = sem("idx_psum")
        idx_sum = sem("idx_sum")
        idx_ready = sem("idx_ready")
        cur_ready = sem("cur_ready")
        gathered = sem("gathered")
        x_transposed = sem("x_transposed")
        xT_ready = sem("xT_ready")
        sel_ready = sem("sel_ready")
        gate_psum = sem("gate_psum")
        up_psum = sem("up_psum")
        gmin_ready = sem("gmin_ready")
        sig_ready = sem("sig_ready")
        gs_ready = sem("gs_ready")
        up_ready = sem("up_ready")
        act_ready = sem("act_ready")
        act_transposed = sem("act_transposed")
        actT0_ready = sem("actT0_ready")
        actT1_ready = sem("actT1_ready")
        y_psum = sem("y_psum")
        y_ready = sem("y_ready")
        scattered = sem("scattered")

        def t_filled(eng, key, half=0):
            b, n = T[(key, half)]
            eng.wait_ge(t_full[b], n + 1)
            return b

        def t_evacuated(eng, key, half=0):
            b, n = T[(key, half)]
            eng.wait_ge(t_free[b], n + 1)

        def head_of(i):
            h = i % HEADS
            return i < HEADS, h, h // 2, HD * (h % 2)

        def keys_of(g):
            t, fox = g // 16, g % 16 < HEADS
            first = 0 if fox or t == 0 else t - 1
            return first, t + 1 - first

        block = ctx.enter_context(nc.Block())

        @block.sync
        def _(sp):
            def load_small(dst, src):
                sp.dma_start(dst, src, allow_slow_non_contiguous=True).then_inc(small_loaded, 16)

            def load_x(t):
                if t >= 2:
                    t_filled(sp, ("hn", t - 2), 1)
                sp.dma_start(xt[:, t % 2, :], x[0, t * P:(t + 1) * P, :]).then_inc(x_loaded[t % 2], 16)

            def load_win(n):
                c = CH[n]
                if n >= 2:
                    b, k = A[(("proj", CH[n - 2], TILES - 1), 0)]
                    sp.wait_ge(a_full[b], k + 1)
                dst = w_buf[n % 2]
                if c == "kvf":
                    sp.dma_start(dst[:, :, 0:2 * KV * HD], w_in[0, :, KB:IN_WIDTH].rearrange("(k p) n -> p k n", p=P)
                                 ).then_inc(win_loaded[0], 16)
                    sp.dma_start(dst[:, :, 2 * KV * HD:KVF], w_in[0, :, FG:QB].rearrange("(k p) n -> p k n", p=P)
                                 ).then_inc(win_loaded[0], 16)
                else:
                    sp.dma_start(dst, w_in[0, :, CH_AT[c]:CH_AT[c] + HW].rearrange("(k p) n -> p k n", p=P)
                                 ).then_inc(win_loaded[n % 2], 16)

            sp.dma_start(rel[0:BUCKETS, :], rel_bias).then_inc(rel_loaded, 16)
            sp.dma_start(tabs, buckets).then_inc(rel_loaded, 16)
            load_x(0)
            load_x(1)
            load_small(gmix[:, :], norm_mix[0].rearrange("(k p) -> p k", p=P))
            for j, g in enumerate((q_norm_fox, k_norm_fox, q_norm_swa, k_norm_swa)):
                for half in range(2):
                    load_small(gcols[half * HD:(half + 1) * HD, j:j + 1], g.rearrange("a d -> d a"))
            load_small(bf_b[:, :], b_forget.broadcast_to([P, HEADS]))
            load_small(sink_b[:, :], sinks.broadcast_to([P, HEADS]))
            load_small(br_b[:, :], b_router.broadcast_to([P, EXPERTS]))
            load_small(wr[:, :, :], w_router[0].rearrange("(k p) n -> p k n", p=P))
            load_win(0)
            load_x(2)
            load_x(3)
            load_win(1)
            for r in range(3):
                rows = slice(EXPERTS * r, EXPERTS * r + EXPERTS)
                sp.dma_start(bias_rest[rows, 0:2 * D], b_up_gate[0]).then_inc(bias_raw, 16)
                sp.dma_start(bias_rest[rows, 2 * D:3 * D], b_down[0]).then_inc(bias_raw, 16)
            for h in (HEADS - 2, HEADS - 1):
                t_evacuated(sp, ("toep", h))
            sp.dma_start(toep_dram, toep_sb).then_inc(toep_stored, 16)
            sp.wait_ge(toep_stored, 16)
            row = HEADS * TOEP
            skew = toep_dram.rearrange("p c -> (p c)")[WINDOW - 1:WINDOW - 1 + P * (row - 1)]
            skew = skew.rearrange("(q c) -> q c", c=row - 1)
            for h in range(HEADS):
                sp.dma_start(swa_bias[:, h, :], skew[:, h * TOEP:h * TOEP + BAND]).then_inc(bias_loaded, 16)
            def load_chunk(c, e):
                dst = ring[:, c * CHUNK_COLS:(c + 1) * CHUNK_COLS].rearrange("p (k n) -> p k n", k=2)
                k = c % 4
                if c < 8:
                    src = w_up_gate[0, e, k * 2 * P:(k + 1) * 2 * P, (c // 4) * D:(c // 4 + 1) * D]
                else:
                    src = w_down[0, e, k * 2 * P:(k + 1) * 2 * P, :]
                return dst, src.rearrange("(k p) n -> p k n", p=P)

            load_win(2)
            for c in range(2, 8):
                sp.dma_start(*load_chunk(c, 0)).then_inc(w_loaded[c], 16)
            load_win(3)
            load_win(4)
            sp.wait_ge(bias_split, 5)
            for c in range(2):
                sp.dma_start(*load_chunk(c, 0)).then_inc(w_loaded[c], 16)
            for n in (3, 4):
                b, k = A[(("proj", CH[n], TILES - 1), 0)]
                sp.wait_ge(a_full[b], k + 1)
            sp.dma_start(wout_sb, w_out[0].rearrange("(k p) n -> p k n", p=P)).then_inc(wout_loaded, 16)
            t_filled(sp, ("turn", "qb", TILES - 1))
            sp.dma_start(gmoe[:, :], norm_moe.broadcast_to([P, D])).then_inc(tail_loaded, 16)
            for t in range(TILES):
                if t:
                    sp.wait_ge(rows_stored, 32 * t)
                    sp.wait_ge(hn2_ready, t)
                sp.dma_start(hb[:, :], x[0, t * P:(t + 1) * P, :]).then_inc(h_in, 16)
                sp.wait_ge(h_ready, 2 * t + 2)
                sp.dma_start(out[t * P:(t + 1) * P, :], hb[:, :]).then_inc(rows_stored, 16)
                sp.wait_ge(hn2_ready, t + 1)
                sp.dma_start(hn2_dram[t * P:(t + 1) * P, :], hn2[:, :]).then_inc(rows_stored, 16)
            sp.dma_start(out[SEQ:OUT_ROWS, :], hn2[:, :]).then_inc(rows_stored, 16)
            b, k = A[(("out1", TILES - 1), 0)]
            sp.wait_ge(a_full[b], k + 1)
            sp.wait_ge(gathered, 16)
            for c in range(8, CHUNKS):
                sp.dma_start(*load_chunk(c, 0)).then_inc(w_loaded[c], 16)

            with sp.Fori(1, EXPERTS) as e:
                for c in range(CHUNKS):
                    sp.wait_ge(chunk_used, e * CHUNKS - (CHUNKS - c - 1))
                    sp.dma_start(*load_chunk(c, e)).then_inc(w_loaded[c], 16)
            sp.wait_ge(over_ready, 1)
            some = sp.value_load(over_tab[0:1, 32:33], min_val=0, max_val=1)
            with sp.If(some > 0):
                with sp.Fori(0, OVER) as j:
                    used = sp.value_load(over_tab[0:1, bass.ds(j + 32, 1)], min_val=0, max_val=1)
                    with sp.If(used > 0):
                        e = sp.value_load(over_tab[0:1, bass.ds(j, 1)], min_val=0, max_val=EXPERTS - 1)
                        for c in range(CHUNKS):
                            sp.wait_ge(chunk_used, (j + EXPERTS) * CHUNKS - (CHUNKS - c - 1))
                            sp.dma_start(*load_chunk(c, e)).then_inc(w_loaded[c], 16)

        @block.gpsimd
        def _(pool):
            g = nc.gpsimd
            for dst, v in ((ident, 0.0), (ident_b, 0.0), (ones, 1.0), (ones_b, 1.0), (tri, 1.0), (before, 1.0),
                           (causal, 0.0), (expert_row, 0.0)):
                g.memset(dst[:, :], v).then_inc(consts, 1)
            g.memset(head_row[:, :, :], 0.0).then_inc(consts, 1)
            g.iota(iota_slot[:, :], pattern=[[1, SEQ]], base=0, channel_multiplier=0,
                   allow_small_or_imprecise_dtypes=True).then_inc(consts, 1)
            g.iota(iota_exp[:, :], pattern=[[1, EXPERTS]], base=0, channel_multiplier=0,
                   allow_small_or_imprecise_dtypes=True).then_inc(consts, 1)
            g.iota(lane[:, :], pattern=[[0, 1]], base=0, channel_multiplier=1,
                   allow_small_or_imprecise_dtypes=True).then_inc(consts, 1)
            g.iota(slot_trash[:, :], pattern=[[0, 1]], base=SEQ, channel_multiplier=1,
                   allow_small_or_imprecise_dtypes=True).then_inc(consts, 1)
            pool.wait_ge(consts, 13)
            for m in (ident, ident_b):
                g.affine_select(out=m[:, :], in_=m[:, :], compare_op=ALU.not_equal, fill=1.0, base=0,
                                pattern=[[-1, P]], channel_multiplier=1).then_inc(masks_built, 1)
            g.affine_select(out=tri[:, :], in_=tri[:, :], compare_op=ALU.is_ge, fill=0.0, base=0,
                            pattern=[[1, P]], channel_multiplier=-1).then_inc(masks_built, 1)
            g.affine_select(out=before[:, :], in_=before[:, :], compare_op=ALU.is_ge, fill=0.0, base=-1,
                            pattern=[[1, P]], channel_multiplier=-1).then_inc(masks_built, 1)
            dia = causal[:, SEQ - P:SEQ]
            g.affine_select(out=dia, in_=dia, compare_op=ALU.is_ge, fill=NEG, base=0,
                            pattern=[[-1, P]], channel_multiplier=1).then_inc(masks_built, 1)
            for part in range(3):
                g.affine_select(out=head_row[:, :, :], in_=head_row[:, :, :], compare_op=ALU.not_equal, fill=1.0,
                                base=-8 * part, pattern=[[-1, HEADS], [0, P]], channel_multiplier=1
                                ).then_inc(masks_built, 1)
                g.affine_select(out=expert_row[:, :], in_=expert_row[:, :], compare_op=ALU.not_equal, fill=1.0,
                                base=-32 * part, pattern=[[-1, EXPERTS]], channel_multiplier=1
                                ).then_inc(masks_built, 1)
                pool.wait_ge(masks_built, 5 + 2 * (part + 1))

            g.memset(ones_f[:, :], 1.0).then_inc(late_consts, 1)
            g.tensor_copy(iota_blk[:, :], iota_slot[:, 0:P]).then_inc(late_consts, 1)
            for j in range(TILES):
                g.memset(idx_rhs[:, j, 0:1], float(P * j - 1024)).then_inc(late_consts, 1)
                g.tensor_copy(idx_rhs[:, j, 1:2], lane[:, :]).then_inc(late_consts, 1)

            pool.wait_ge(bias_raw, 16 * 6)
            g.tensor_copy(bias_tab[:, :], bias_rest).then_inc(bias_split, 1)
            for n, part in enumerate((2 * EXPERTS, EXPERTS)):
                pool.wait_ge(bias_split, 2 * n + 1)
                g.tensor_tensor(bias_rest[0:part], bias_rest[0:part], bias_tab[0:part, :], ALU.subtract
                                ).then_inc(bias_split, 1)
                pool.wait_ge(bias_split, 2 * n + 2)
                g.tensor_copy(bias_tab[0:part, :], bias_rest[0:part]).then_inc(bias_split, 1)

            pool.wait_ge(score_done, 16 * (TILES - 1) + HEADS)
            g.memset(gx[:, :], 0.0).then_inc(late_consts, 1)
            pool.wait_ge(placed, 1)
            pool.wait_ge(late_consts, 3 + 2 * TILES)

            def value(n):
                return n if isinstance(n, int) else pool.to_reg(n)

            def columns(s, e):
                if later(s):
                    pool.wait_ge(idx_psum, s)
                g.tensor_copy(poscol[:, :].unsqueeze(2), posm[:, :, bass.ds(e, 1)]).then_inc(cols_copied, 1)
                g.tensor_copy(idx_rhs[:, :, 2:5].unsqueeze(2), gate_parts[:, :, bass.ds(e, 1), :]
                              ).then_inc(cols_copied, 1)
                if not later(s):
                    return
                copied = value(2 * s + 2)
                pool.wait_ge(consts, 13)
                pool.wait_ge(cols_copied, copied)
                for j in range(TILES):
                    last = g.tensor_scalar(slot_oh[:, j, :], iota_blk[:, :], poscol[:, j:j + 1], None, ALU.is_equal)
                    last.then_inc(onehot_ready, 1)

            def gather(s):
                pool.wait_ge(consts, 13)
                pool.wait_ge(idx_ready, s * 2 + 2)
                if later(s):
                    pool.wait_ge(x_transposed, s)
                pool.indirect_dma_start(
                    out=gx[:, :], out_offset=None, in_=hn2_dram,
                    in_offset=bass.IndirectOffsetOnAxis(ap=gidx[:, 0:1], axis=0),
                    bounds_check=SEQ - 1, oob_is_err=False).then_inc(gathered, 16)

            def select_bias(t, e):
                if later(t):
                    pool.wait_ge(y_psum, t)
                g.tensor_copy(bias_sel[:, :], expert_row[:, bass.ds(e, 1)].broadcast_to([96, P])
                              ).then_inc(sel_ready, 1)

            def scatter(t):
                results, current, before_it = value(t + 1), value(2 * t + 2), value(t * 16)
                pool.wait_ge(consts, 13)
                pool.wait_ge(y_ready, results)
                pool.wait_ge(cur_ready, current)
                if later(t):
                    pool.wait_ge(scattered, before_it)
                pool.indirect_dma_start(
                    out=out, out_offset=bass.IndirectOffsetOnAxis(ap=sidx[:, 0:1], axis=0),
                    in_=y_sb[:, :], in_offset=None, compute_op=ALU.add).then_inc(scattered, 16)

            pool.wait_ge(rows_stored, 16 * (2 * TILES + 1))
            gather(0)
            pool.wait_ge(gates_ready, TILES)
            columns(0, 0)
            select_bias(0, 0)
            columns(1, 1)
            gather(1)
            scatter(0)
            with pool.Fori(1, EXPERTS - 1) as t:
                select_bias(t, t)
                columns(t + 1, t + 1)
                gather(t + 1)
                scatter(t)
            select_bias(EXPERTS - 1, EXPERTS - 1)
            scatter(EXPERTS - 1)
            pool.wait_ge(scattered, 16 * EXPERTS)
            pool.wait_ge(over_ready, 1)
            some = pool.value_load(over_tab[0:1, 32:33], min_val=0, max_val=1)
            with pool.If(some > 0):
                with pool.Fori(0, OVER) as j:
                    used = pool.value_load(over_tab[0:1, bass.ds(j + 32, 1)], min_val=0, max_val=1)
                    with pool.If(used > 0):
                        e = pool.value_load(over_tab[0:1, bass.ds(j, 1)], min_val=0, max_val=EXPERTS - 1)
                        rank = pool.value_load(over_tab[0:1, bass.ds(j + 16, 1)], min_val=0, max_val=TILES - 1)
                        t = j + EXPERTS
                        pool.wait_ge(idx_psum, t)
                        g.tensor_copy(iota_blk[:, :], iota_slot[:, bass.ds(rank * P, P)]).then_inc(late_consts, 1)
                        pool.wait_ge(late_consts, j + (4 + 2 * TILES))
                        columns(t, e)
                        gather(t)
                        select_bias(t, e)
                        scatter(t)
                        pool.wait_ge(scattered, t * 16 + 16)

        @block.scalar
        def _(act):
            a = nc.scalar

            def root(dst, src, eps):
                a.activation(dst, src, ACT.Sqrt, bias=eps).then_inc(rs_ready, 1)

            act.wait_ge(eps_ready, 2)

            def xn(t):
                act.wait_ge(x_loaded[t % 2], 16 * (t // 2 + 1))
                a.activation(s_sb[:, :, :].rearrange("p a n -> p (a n)"), xt[:, t % 2, :], ACT.Square,
                             accum_out=ssx[:, t:t + 1]).then_inc(xn_sq, 1)
                act.wait_ge(xn_sq, t + 1)
                root(rsx[:, t:t + 1], ssx[:, t:t + 1], eps_d[:, :])

            def proj(c, t):
                b, k = A[(("proj", c, t), 0)]
                act.wait_ge(a_full[b], k + 1)
                if c == "va":
                    a.copy(va[:, t, :], acc_ps[b][:, :]).then_inc(va_ready, 1)
                    return
                n = NORMED.index(c) * TILES + t
                w = HW if c != "kvf" else KV * HD
                if n:
                    act.wait_ge(sq_free, n)
                a.activation(sq[:, 0:w], acc_ps[b][:, 0:w], ACT.Square).then_inc(sq_ready, 1)
                heads = HEADS if c != "kvf" else KV
                act.wait_ge(sq_free, n + 1)
                root(rs[:, 0:heads], ss[:, 0:heads], eps_h[:, :])

            def turn(c, t):
                b = t_filled(act, ("turn", c, t))
                cols = slice(t * P, (t + 1) * P)
                dst, j, m = {"qa": (qaT, 0, 4), "ka": (kaT, 1, 4), "qb": (qbT, 2, 4), "kvf": (kbT, 3, 2)}[c]
                act.wait_ge(gcols_ready, 2)
                a.activation(dst[:, :, cols], t_ps[b][:, 0:m * P].rearrange("p (m n) -> p m n", m=m), ACT.Copy,
                             scale=gcols[:, j:j + 1]).then_inc(t_free[b], 1)

            def forget():
                act.wait_ge(f_ready, 1)
                a.activation(ze[:, :, :], za[:, :, :], ACT.Exp, scale=-1.0).then_inc(f_log, 1)
                act.wait_ge(f_log, 1)
                a.activation(ze[:, :, :], ze[:, :, :], ACT.Ln, bias=1.0).then_inc(f_log, 1)

            def score(g):
                t, i = divmod(g, 16)
                _, n = keys_of(g)
                act.wait_ge(score_ready, g + 1)
                if g >= 2:
                    t_filled(act, ("probs", g - 2))
                if i == 0 and t >= 2:
                    act.wait_ge(mix_ready, 2 * t - 2)
                a.activation(p_sb[:, g % 2, 0:n * P], s_sb[:, g % 2, 0:n * P], ACT.Exp, scale=-1.0,
                             bias=negm[:, t % 2, i:i + 1], accum_out=den[:, t % 2, i:i + 1]).then_inc(probs_ready, 1)

            def probs(g):
                if g % 2 == 0:
                    return
                _, n = keys_of(g)
                b = t_filled(act, ("probs", g))
                if g >= 2:
                    act.wait_ge(value_done, g - 1)
                a.copy(pT[:, g % 2, 0:n * P], t_ps[b][:, 0:n * P]).then_inc(t_free[b], 1)

            def value(g):
                t, i = divmod(g, 16)
                if i == 15:
                    act.wait_ge(sink_in, t + 1)
                    a.activation(sk[:, 1, :], sk[:, 0, :], ACT.Exp).then_inc(sink_exp, 1)

            def mix(t):
                b = t_filled(act, ("mix", t), 1)
                a.copy(mixT[:, 4:8, :], t_ps[b][:, :].rearrange("p (m n) -> p m n", m=4)).then_inc(t_free[b], 1)

            def squares0(t):
                if t == TILES - 1:
                    a.activation(spare[:, :], eps_d[:, :], ACT.Sqrt)
                act.wait_ge(h_ready, 2 * t + 1)
                if t:
                    act.wait_ge(rows_stored, 32 * t)
                    t_filled(act, ("hn2", t - 1), 1)
                    act.wait_ge(hn2_ready, t)
                a.activation(hn2[:, 0:HALF], hb[:, 0:HALF], ACT.Square, accum_out=ss2[:, 0:1]).then_inc(h_sq, 1)

            def squares1(t):
                act.wait_ge(h_ready, 2 * t + 2)
                a.activation(hn2[:, HALF:D], hb[:, HALF:D], ACT.Square, accum_out=ss2[:, 1:2]).then_inc(h_sq, 1)
                act.wait_ge(h_sq, 3 * t + 2)
                a.activation(ss2[:, 0:1], ss2[:, 0:1], ACT.Identity, bias=eps_d[:, :]).then_inc(h_sq, 1)
                act.wait_ge(h_sq, 3 * t + 3)
                root(ss2[:, 1:2], ss2[:, 1:2], ss2[:, 0:1])

            def hn2_(t):
                b = t_filled(act, ("hn2", t), 1)
                a.copy(hn2T[:, 4:8, :], t_ps[b][:, :].rearrange("p (m n) -> p m n", m=4)).then_inc(t_free[b], 1)

            def route(t):
                act.wait_ge(ntop_ready, t + 1)
                a.activation(ex[:, :], top[:, 0:TOPK], ACT.Exp, bias=ntop[:, :], accum_out=exs[:, 0:1]
                             ).then_inc(ex_ready, 1)

            does = {"xn": xn, "proj": proj, "turn": turn, "forget": forget, "score": score, "probs": probs,
                    "value": value, "mix": mix, "squares0": squares0, "squares1": squares1, "hn2": hn2_, "route": route}
            for s in order:
                if s[0] in does:
                    does[s[0]](*s[1:])

            def rows_in(s):
                act.wait_ge(x_transposed, s + 1)
                for half in range(2):
                    a.copy(xT[:, 4 * half:4 * half + 4, :], gate_ps[half][:, :].rearrange("p (m n) -> p m n", m=4)
                           ).then_inc(xT_ready, 1)

            def expert(t, ahead):
                act.wait_ge(gmin_ready, t + 1)
                if later(t):
                    act.wait_ge(gs_ready, t)
                a.activation(sig[:, :], gmin[:, :], ACT.Sigmoid, scale=ALPHA).then_inc(sig_ready, 1)
                act.wait_ge(act_transposed, t * 2 + 1)
                if later(t):
                    act.wait_ge(y_psum, t)
                a.copy(actT[:, 0:4, :], turn_ps[0][:, :].rearrange("p (m n) -> p m n", m=4)
                       ).then_inc(actT0_ready, 1)
                if ahead:
                    rows_in(t + 1)
                act.wait_ge(y_psum, t + 1)
                act.wait_ge(cur_ready, t * 2 + 2)
                if later(t):
                    act.wait_ge(scattered, t * 16)
                for half in range(2):
                    last = a.activation(y_sb[:, half * HALF:(half + 1) * HALF], y_ps[half][:, :], ACT.Copy,
                                        scale=gate[:, 0:1])
                last.then_inc(y_ready, 1)

            rows_in(0)
            expert(0, True)
            with act.Fori(1, EXPERTS - 1) as t:
                expert(t, True)
            expert(EXPERTS - 1, False)
            act.wait_ge(over_ready, 1)
            some = act.value_load(over_tab[0:1, 32:33], min_val=0, max_val=1)
            with act.If(some > 0):
                with act.Fori(0, OVER) as j:
                    used = act.value_load(over_tab[0:1, bass.ds(j + 32, 1)], min_val=0, max_val=1)
                    with act.If(used > 0):
                        rows_in(j + EXPERTS)
                        expert(j + EXPERTS, False)

        @block.vector
        def _(dve):
            v = nc.vector
            steps = [0]

            def link(ins):
                ins.then_inc(step, 1)
                steps[0] += 1
                dve.wait_ge(step, steps[0])

            v.memset(eps_d[:, :], D * EPS).then_inc(eps_ready, 1)
            v.memset(eps_h[:, :], HD * EPS).then_inc(eps_ready, 1)
            link(v.memset(rel[BUCKETS:BUCKETS + 1, :], 1.0))
            dve.wait_ge(rel_loaded, 32)
            v.tensor_copy(lams, rel[:, :].unsqueeze(2).broadcast_to([BUCKETS + 1, HEADS, P])).then_inc(lams_ready, 1)

            def xn(t):
                dve.wait_ge(rs_ready, t + 1)
                link(v.reciprocal(rsx[:, t:t + 1], rsx[:, t:t + 1]))
                v.tensor_scalar(xt[:, t % 2, :], xt[:, t % 2, :], rsx[:, t:t + 1], None, ALU.mult).then_inc(xn_ready, 1)

            def hn(t):
                if t == 0:
                    dve.wait_ge(small_loaded, 16 * 13)
                    link(v.tensor_scalar(gmix[:, :], gmix[:, :], D ** 0.5, None, ALU.mult))
                for half in range(2):
                    b = t_filled(dve, ("hn", t), half)
                    v.tensor_tensor(hnT[:, 4 * half:4 * half + 4, t * P:(t + 1) * P],
                                    t_ps[b][:, :].rearrange("p (m n) -> p m n", m=4),
                                    gmix[:, 4 * half:4 * half + 4].unsqueeze(2).broadcast_to([P, 4, P]),
                                    ALU.mult).then_inc(t_free[b], 1)
                if t == 0:
                    for j in (1, 3):
                        v.tensor_scalar(gcols[:, j:j + 1], gcols[:, j:j + 1], HD ** 0.5, None, ALU.mult
                                        ).then_inc(gcols_ready, 1)
                    v.tensor_scalar(nsink[:, :], sink_b[:, :], -1.0, None, ALU.mult).then_inc(step, 1)
                    steps[0] += 1

            def toep(h):
                b = t_filled(dve, ("toep", h))
                v.tensor_copy(toep_sb[:, h * TOEP:(h + 1) * TOEP], t_ps[b][:, 0:TOEP]).then_inc(t_free[b], 1)

            def proj(c, t):
                if c == "va":
                    return
                b, _ = A[(("proj", c, t), 0)]
                n = NORMED.index(c) * TILES + t
                hn_ = HEADS if c != "kvf" else KV
                w = hn_ * HD
                dve.wait_ge(sq_ready, n + 1)
                v.tensor_reduce(ss[:, 0:hn_], sq[:, 0:w].rearrange("p (h d) -> p h d", d=HD), AX.X, ALU.add
                                ).then_inc(sq_free, 1)
                dve.wait_ge(rs_ready, TILES + n + 1)
                link(v.reciprocal(rs[:, 0:hn_], rs[:, 0:hn_]))
                if n >= 2:
                    c2, t2 = NORMED[(n - 2) // TILES], (n - 2) % TILES
                    t_filled(dve, ("turn", c2, t2))
                src = acc_ps[b][:, 0:w].rearrange("p (h d) -> p h d", d=HD)
                r = rs[:, 0:hn_].unsqueeze(2).broadcast_to([P, hn_, HD])
                if c == "kvf":
                    dst = qn[:, n % 2, 0:2 * w].rearrange("p (h u d) -> p u h d", u=2, d=HD)
                    v.tensor_tensor(dst[:, 0, :, :], src, r, ALU.mult).then_inc(qn_ready, 1)
                    v.tensor_tensor(dst[:, 1, :, :], src, r, ALU.mult).then_inc(qn_ready, 1)
                    v.tensor_copy(vb[:, t, :], acc_ps[b][:, KV * HD:2 * KV * HD]).then_inc(vb_ready, 1)
                    v.tensor_tensor(zf[:, t, :], acc_ps[b][:, 2 * KV * HD:KVF], bf_b[:, :], ALU.add
                                    ).then_inc(zf_ready, 1)
                    if t == TILES - 1:
                        dve.wait_ge(zf_ready, TILES)
                        link(v.tensor_scalar(za[:, :, :], zf[:, :, :], -1.0, None, ALU.mult))
                        v.tensor_tensor(za[:, :, :], za[:, :, :], zf[:, :, :], ALU.max).then_inc(f_ready, 1)
                else:
                    v.tensor_tensor(qn[:, n % 2, :].rearrange("p (h d) -> p h d", d=HD), src, r, ALU.mult
                                    ).then_inc(qn_ready, 1)

            def forget():
                dve.wait_ge(f_log, 2)
                v.scalar_tensor_tensor(out=logf[:, :, :], in0=zf[:, :, :], scalar=0.0, in1=ze[:, :, :],
                                       op0=ALU.min, op1=ALU.subtract).then_inc(logf_ready, 1)

            def decay():
                b = t_filled(dve, ("decay",))
                v.tensor_copy(csum[:, :, :], t_ps[b][:, 0:TILES * HEADS].rearrange("p (t h) -> p t h", h=HEADS)
                              ).then_inc(t_free[b], 1)
                dve.wait_ge(t_free[b], T[(("decay",), 0)][1] + 1)
                link(v.tensor_copy(cpart[:, :, 0, :], csum[:, :, :]))
                link(v.tensor_tensor(crest[:, :, :], csum[:, :, :], cpart[:, :, 0, :], ALU.subtract))
                link(v.tensor_copy(cpart[:, :, 1, :], crest[:, :, :]))
                link(v.tensor_tensor(crest[:, :, :], crest[:, :, :], cpart[:, :, 1, :], ALU.subtract))
                v.tensor_copy(cpart[:, :, 2, :], crest[:, :, :]).then_inc(cpart_ready, 1)

            def decay_turn():
                b = t_filled(dve, ("decay_turn",))
                src = t_ps[b][0:24, 0:SEQ // 2].bitcast(BF16)
                v.tensor_copy(cT[:, :], src).then_inc(ct_ready, 1)
                v.tensor_scalar(ncT[:, :], src, -1.0, None, ALU.mult).then_inc(t_free[b], 1)

            def score(g):
                t, i = divmod(g, 16)
                fox, h, _, _ = head_of(i)
                _, n = keys_of(g)
                dve.wait_ge(score_done, g + 1)
                if g == 0:
                    dve.wait_ge(masks_built, 11)
                if g == HEADS:
                    dve.wait_ge(bias_loaded, 16 * HEADS)
                if g >= 2:
                    dve.wait_ge(probs_ready, g - 1)
                if i == 0 and t >= 2:
                    dve.wait_ge(sink_exp, t - 1)
                add = causal[:, SEQ - n * P:SEQ] if fox else swa_bias[:, h, BAND - n * P:BAND]
                v.tensor_tensor_reduce(out=s_sb[:, g % 2, 0:n * P], in0=s_ps[g % 2][:, 0:n * P], in1=add, scale=-1.0,
                                       scalar=-NEG if fox else nsink[:, h:h + 1], op0=ALU.add, op1=ALU.min,
                                       accum_out=negm[:, t % 2, i:i + 1]).then_inc(score_ready, 1)

            def probs(g):
                if g % 2:
                    return
                _, n = keys_of(g)
                b = t_filled(dve, ("probs", g))
                if g >= 2:
                    dve.wait_ge(value_done, g - 1)
                v.tensor_copy(pT[:, g % 2, 0:n * P], t_ps[b][:, 0:n * P]).then_inc(t_free[b], 1)

            def value(g):
                t, i = divmod(g, 16)
                if i == 13:
                    dve.wait_ge(score_ready, 16 * t + 16)
                    if t:
                        dve.wait_ge(sink_exp, t)
                    v.tensor_tensor(sk[:, 0, :], sink_b[:, :], negm[:, t % 2, HEADS:], ALU.add).then_inc(sink_in, 1)

            def norm(t, group):
                fox, lo = group == 0, group * HEADS
                dve.wait_ge(value_done, 16 * t + lo + HEADS)
                dve.wait_ge(probs_ready, 16 * t + lo + HEADS)
                d = den[:, t % 2, lo:lo + HEADS]
                if not fox:
                    dve.wait_ge(sink_exp, t + 1)
                    link(v.tensor_tensor(d, d, sk[:, 1, :], ALU.add))
                link(v.reciprocal(rden[:, lo:lo + HEADS], d))
                if t:
                    t_filled(dve, ("mix", t - 1), 1)
                elif fox:
                    t_filled(dve, ("turn", "qb", TILES - 1))
                v.tensor_tensor(o_sb[:, lo * HD:(lo + HEADS) * HD].rearrange("p (h d) -> p h d", d=HD),
                                o_ps[group][:, :].rearrange("p (h d) -> p h d", d=HD),
                                rden[:, lo:lo + HEADS].unsqueeze(2).broadcast_to([P, HEADS, HD]),
                                ALU.mult).then_inc(mix_ready, 1)

            def mix(t):
                b = t_filled(dve, ("mix", t), 0)
                v.tensor_copy(mixT[:, 0:4, :], t_ps[b][:, :].rearrange("p (m n) -> p m n", m=4)).then_inc(t_free[b], 1)

            def residual(n, t):
                b, k = A[((f"out{n}", t), 0)]
                dve.wait_ge(a_full[b], k + 1)
                dve.wait_ge(h_in, 16 * (t + 1))
                half = hb[:, n * HALF:(n + 1) * HALF]
                v.tensor_tensor(half, acc_ps[b][:, :], half, ALU.add).then_inc(h_ready, 1)

            def norm2(t):
                if t == 0:
                    dve.wait_ge(tail_loaded, 16)
                    link(v.tensor_scalar(gmoe[:, :], gmoe[:, :], D ** 0.5, None, ALU.mult))
                dve.wait_ge(rs_ready, TILES * (2 + len(NORMED)) - (TILES - 1 - t))
                link(v.reciprocal(ss2[:, 1:2], ss2[:, 1:2]))
                v.scalar_tensor_tensor(out=hn2[:, :], in0=hb[:, :], scalar=ss2[:, 1:2], in1=gmoe[:, :],
                                       op0=ALU.mult, op1=ALU.mult).then_inc(hn2_ready, 1)

            def hn2_(t):
                b = t_filled(dve, ("hn2", t), 0)
                v.tensor_copy(hn2T[:, 0:4, :], t_ps[b][:, :].rearrange("p (m n) -> p m n", m=4)).then_inc(t_free[b], 1)

            def route(t):
                b = t_filled(dve, ("route", t))
                v.tensor_tensor(lg[:, :], t_ps[b][:, 0:EXPERTS], br_b[:, :], ALU.add).then_inc(t_free[b], 1)
                dve.wait_ge(t_free[b], T[(("route", t), 0)][1] + 1)
                link(v.max(top[:, :], lg[:, :]))
                v.tensor_scalar(ntop[:, :], top[:, 0:1], -1.0, None, ALU.mult).then_inc(ntop_ready, 1)
                link(v.max_index(topi[:, :], top[:, :], lg[:, :]))
                link(v.tensor_copy(topf[:, :], topi[:, 0:TOPK]))
                link(v.tensor_tensor(eq[:, :, :], iota_exp[:, :].unsqueeze(1).broadcast_to([P, TOPK, EXPERTS]),
                                     topf[:, :].unsqueeze(2).broadcast_to([P, TOPK, EXPERTS]), ALU.is_equal))
                link(v.tensor_reduce(mask[:, t, :], eq[:, :, :].rearrange("p k e -> p e k"), AX.X, ALU.add))
                v.tensor_copy(mask_b[:, t, :], mask[:, t, :]).then_inc(mask_ready, 1)

            def gates(t):
                dve.wait_ge(ex_ready, t + 1)
                link(v.reciprocal(exs[:, 1:2], exs[:, 0:1]))
                link(v.tensor_scalar(ex[:, :], ex[:, :], exs[:, 1:2], None, ALU.mult))
                if t:
                    dve.wait_ge(gates_ready, t)
                link(v.tensor_tensor(eqg[:, :, :], eq[:, :, :], ex[:, :].unsqueeze(2).broadcast_to([P, TOPK, EXPERTS]),
                                     ALU.mult))
                link(v.tensor_reduce(gsum[:, :], eqg[:, :, :].rearrange("p k e -> p e k"), AX.X, ALU.add))
                link(v.tensor_copy(gate_parts[:, t, :, 0], gsum[:, :]))
                link(v.tensor_tensor(gsum[:, :], gsum[:, :], gate_parts[:, t, :, 0], ALU.subtract))
                link(v.tensor_copy(gate_parts[:, t, :, 1], gsum[:, :]))
                link(v.tensor_tensor(gsum[:, :], gsum[:, :], gate_parts[:, t, :, 1], ALU.subtract))
                v.tensor_copy(gate_parts[:, t, :, 2], gsum[:, :]).then_inc(gates_ready, 1)

            def place():
                b = t_filled(dve, ("place",))
                link(v.scalar_tensor_tensor(
                    out=posm[:, :, :], in0=t_ps[b][:, 0:TILES * EXPERTS].rearrange("p (t e) -> p t e", e=EXPERTS),
                    scalar=1.0, in1=mask[:, :, :], op0=ALU.add, op1=ALU.mult))
                link(v.tensor_scalar(posm[:, :, :], posm[:, :, :], -1.0, None, ALU.add))
                v.tensor_tensor(slot_oh[:, :, :], iota_slot[:, 0:P].unsqueeze(1).broadcast_to([P, TILES, P]),
                                posm[:, :, 0:1].broadcast_to([P, TILES, P]), ALU.is_equal
                                ).then_inc(onehot_ready, TILES)
                dve.wait_ge(rows_stored, 16 * (2 * TILES + 1))
                v.tensor_copy(ocnt[:, :], t_ps[b][0:EXPERTS, 128:129]).then_inc(placed, 1)

            def tokens():
                dve.wait_ge(tok_psum, 1)
                v.tensor_reduce(tokf[:, :], gate_ps[0][:, 0:2], AX.X, ALU.add).then_inc(idx_sum, 1)
                dve.wait_ge(idx_sum, 1)
                slots(0)

            def slots(s):
                v.tensor_scalar(sidx_next[:, :], tokf[:, :], 1024.0, slot_trash[:, 0:1], ALU.add, ALU.min
                                ).then_inc(idx_ready, 1)
                v.tensor_scalar(gidx[:, :], tokf[:, :], 1024.0, None, ALU.add).then_inc(idx_ready, 1)

            does = {"xn": xn, "hn": hn, "toep": toep, "proj": proj, "forget": forget, "decay": decay,
                    "decay_turn": decay_turn, "score": score, "probs": probs, "value": value, "mix": mix,
                    "out0": lambda t: residual(0, t), "out1": lambda t: residual(1, t),
                    "hn2": hn2_, "route": route, "gates": gates, "place": place, "tokens": tokens, "norm": norm, "norm2": norm2}
            for s in order:
                if s[0] in does:
                    does[s[0]](*s[1:])

            def indices(s):
                dve.wait_ge(idx_psum, s + 1)
                dve.wait_ge(cur_ready, s * 2)
                v.tensor_reduce(tokf[:, :], gate_ps[0][:, 0:2], AX.X, ALU.add).then_inc(idx_sum, 1)
                v.tensor_reduce(gate_next[:, :], gate_ps[0][:, 2:5], AX.X, ALU.add).then_inc(idx_sum, 1)
                dve.wait_ge(idx_sum, s * 2 + 2)
                dve.wait_ge(gathered, s * 16)
                slots(s)

            def current(t):
                dve.wait_ge(idx_ready, t * 2 + 2)
                if later(t):
                    dve.wait_ge(y_ready, t)
                    dve.wait_ge(scattered, t * 16)
                v.tensor_copy(gate[:, :], gate_next[:, :]).then_inc(cur_ready, 1)
                v.tensor_copy(sidx[:, :], sidx_next[:, :]).then_inc(cur_ready, 1)

            def swiglu_gate(t):
                dve.wait_ge(gate_psum, t + 1)
                if later(t):
                    dve.wait_ge(sig_ready, t)
                for half in range(2):
                    c = slice(half * HALF, (half + 1) * HALF)
                    last = v.tensor_scalar(gmin[:, c], gate_ps[half][:, :], LIMIT, None, ALU.min)
                last.then_inc(gmin_ready, 1)

            def swiglu_rest(t):
                dve.wait_ge(sig_ready, t + 1)
                dve.wait_ge(gmin_ready, t + 1)
                v.tensor_tensor(gs[:, :], gmin[:, :], sig[:, :], ALU.mult).then_inc(gs_ready, 1)
                for half in range(2):
                    c = slice(half * HALF, (half + 1) * HALF)
                    dve.wait_ge(up_psum, t * 2 + half + 1)
                    v.tensor_scalar(up[:, c], up_ps[half][:, :], LIMIT, -LIMIT, ALU.min, ALU.max).then_inc(up_ready, 1)
                    if half == 0:
                        dve.wait_ge(gs_ready, t + 1)
                    dve.wait_ge(up_ready, t * 2 + half + 1)
                    if later(t) and half == 0:
                        dve.wait_ge(act_transposed, t * 2)
                    v.scalar_tensor_tensor(out=act_sb[:, c], in0=up[:, c], scalar=1.0, in1=gs[:, c],
                                           op0=ALU.add, op1=ALU.mult).then_inc(act_ready, 1)
                dve.wait_ge(act_transposed, t * 2 + 2)
                v.tensor_copy(actT[:, 4:8, :], turn_ps[1][:, :].rearrange("p (m n) -> p m n", m=4)
                              ).then_inc(actT1_ready, 1)

            def expert(t, ahead):
                current(t)
                swiglu_gate(t)
                if ahead:
                    indices(t + 1)
                swiglu_rest(t)

            dve.wait_ge(idx_psum, 1)
            v.tensor_reduce(gate_next[:, :], up_ps[0][:, 2:5], AX.X, ALU.add).then_inc(idx_sum, 1)
            dve.wait_ge(idx_sum, 2)
            dve.wait_ge(placed, 1)
            link(v.tensor_scalar(oext[:, :], ocnt[:, :], float(P), None, ALU.is_gt))
            for r in (2, 3):
                link(v.scalar_tensor_tensor(out=oext[:, :], in0=ocnt[:, :], scalar=float(r * P), in1=oext[:, :],
                                            op0=ALU.is_gt, op1=ALU.add))
            v.tensor_copy(oext_b[:, :], oext[:, :]).then_inc(over_step, 1)
            dve.wait_ge(over_pe, 1)
            link(v.tensor_copy(ostart[:, :], y_ps[0][0:EXPERTS, 0:1]))
            link(v.tensor_scalar(odif[:, :], iota_slot[0:32, 0:16], ostart[:, 0:1], None, ALU.subtract))
            link(v.tensor_scalar(ooh[:, 0, :], odif[:, :], 0.0, None, ALU.is_ge))
            link(v.scalar_tensor_tensor(out=ooh[:, 2, :], in0=odif[:, :], scalar=oext[:, 0:1], in1=ooh[:, 0, :],
                                        op0=ALU.is_lt, op1=ALU.mult))
            link(v.scalar_tensor_tensor(out=ooh[:, 1, :], in0=odif[:, :], scalar=1.0, in1=ooh[:, 2, :],
                                        op0=ALU.add, op1=ALU.mult))
            v.tensor_scalar(ooh[:, 0, :], ooh[:, 2, :], lane[0:32, 0:1], None, ALU.mult).then_inc(over_step, 1)
            dve.wait_ge(over_pe, 2)
            v.tensor_copy(over_tab[:, :], y_ps[1][0:1, 0:48]).then_inc(over_ready, 1)

            expert(0, True)
            with dve.Fori(1, EXPERTS - 1) as t:
                expert(t, True)
            expert(EXPERTS - 1, False)
            dve.wait_ge(over_ready, 1)
            some = dve.value_load(over_tab[0:1, 32:33], min_val=0, max_val=1)
            with dve.If(some > 0):
                with dve.Fori(0, OVER) as j:
                    used = dve.value_load(over_tab[0:1, bass.ds(j + 32, 1)], min_val=0, max_val=1)
                    with dve.If(used > 0):
                        indices(j + EXPERTS)
                        expert(j + EXPERTS, False)

        @block.tensor
        def _(pe):
            def t_claim(key, half=0):
                b, n = T[(key, half)]
                if n:
                    pe.wait_ge(t_free[b], n)
                return b

            held = {}

            def a_claim(key):
                b, n = A[(key, 0)]
                if n:
                    last = held[b]
                    t = last[-1]
                    if last[0] != "proj":
                        pe.wait_ge(h_ready, 2 * t + int(last[0][-1]) + 1)
                    elif last[1] == "va":
                        pe.wait_ge(va_ready, t + 1)
                    elif last[1] == "kvf":
                        pe.wait_ge(vb_ready, t + 1)
                        pe.wait_ge(zf_ready, t + 1)
                    else:
                        pe.wait_ge(qn_ready, NORMED.index(last[1]) * TILES + t + 1 + TILES)
                held[b] = key
                return b

            def hn(t):
                pe.wait_ge(xn_ready, t + 1)
                if t == 0:
                    pe.wait_ge(masks_built, 11)
                for half in range(2):
                    b = t_claim(("hn", t), half)
                    for m in range(4):
                        k = 4 * half + m
                        last = pe.transpose(t_ps[b][:, m * P:(m + 1) * P], xt[:, t % 2, k * P:(k + 1) * P], ident[:, :])
                    last.then_inc(t_full[b], 1)

            def toep(h):
                if h == 0:
                    pe.wait_ge(lams_ready, 1)
                b = t_claim(("toep", h))
                pe.matmul(t_ps[b][:, 0:TOEP], lams[:, h, :], tabs, start=True, stop=True).then_inc(t_full[b], 1)

            def proj(c, t):
                n = CH.index(c)
                if t == 0:
                    loads = [32, 16, 48, 32, 64]
                    pe.wait_ge(win_loaded[n % 2], loads[n])
                    if n == 0:
                        for u in range(TILES):
                            for half in range(2):
                                t_evacuated(pe, ("hn", u), half)
                w = HW if c != "kvf" else KVF
                b = a_claim(("proj", c, t))
                for k in range(KT):
                    last = pe.matmul(acc_ps[b][:, 0:w], hnT[:, k, t * P:(t + 1) * P], w_buf[n % 2][:, k, 0:w],
                                     start=(k == 0), stop=(k == KT - 1))
                last.then_inc(a_full[b], 1)

            def turn(c, t):
                n = NORMED.index(c) * TILES + t
                pe.wait_ge(qn_ready, 2 * (n + 1) if c == "kvf" else n + 1 + TILES)
                b = t_claim(("turn", c, t))
                m_ = 2 if c == "kvf" else 4
                for m in range(m_):
                    last = pe.transpose(t_ps[b][:, m * P:(m + 1) * P], qn[:, n % 2, m * P:(m + 1) * P], ident[:, :])
                last.then_inc(t_full[b], 1)

            def decay():
                pe.wait_ge(logf_ready, 1)
                b = t_claim(("decay",))
                for t in range(TILES):
                    dst = t_ps[b][:, t * HEADS:(t + 1) * HEADS]
                    for s in range(t):
                        pe.matmul(dst, ones[:, :], logf[:, s, :], start=(s == 0), stop=False)
                    last = pe.matmul(dst, tri[:, :], logf[:, t, :], start=(t == 0), stop=True)
                last.then_inc(t_full[b], 1)

            def decay_turn():
                pe.wait_ge(cpart_ready, 1)
                b = t_claim(("decay_turn",))
                dst = t_ps[b][0:24, 0:SEQ // 2].bitcast(BF16)
                for t in range(TILES):
                    last = pe.transpose(dst[:, t * P:(t + 1) * P], cpart[:, t, :, :].rearrange("p a h -> p (a h)"),
                                        ident_b[:, :])
                last.then_inc(t_full[b], 1)

            def score(g):
                t, i = divmod(g, 16)
                fox, h, pair, base = head_of(i)
                first, n = keys_of(g)
                if g == 0:
                    for s in (("turn", "ka", TILES - 1), ("turn", "qa", TILES - 1), ("decay_turn",)):
                        t_evacuated(pe, s)
                    for u in range(TILES):
                        t_evacuated(pe, ("turn", "qa", u))
                    pe.wait_ge(ct_ready, 1)
                if g == HEADS:
                    for u in range(TILES):
                        t_evacuated(pe, ("turn", "qb", u))
                if g >= 2:
                    pe.wait_ge(score_ready, g - 1)
                dst = s_ps[g % 2][:, 0:n * P]
                q = (qaT if fox else qbT)[base:base + HD, pair, t * P:(t + 1) * P]
                k = (kaT[base:base + HD, pair, 0:n * P] if fox
                     else kbT[base:base + HD, h // GROUP, first * P:(first + n) * P])
                last = pe.matmul(dst, q, k, start=True, stop=not fox)
                if fox:
                    pe.matmul(dst, head_row[:, h, :], ncT[:, 0:n * P], start=False, stop=False)
                    last = pe.matmul(dst, cT[:, t * P:(t + 1) * P],
                                     head_row[:, h, :].unsqueeze(1).broadcast_to([24, n, P]),
                                     start=False, stop=True)
                last.then_inc(score_done, 1)

            def probs(g):
                _, n = keys_of(g)
                pe.wait_ge(probs_ready, g + 1)
                b = t_claim(("probs", g))
                for m in range(n):
                    last = pe.transpose(t_ps[b][:, m * P:(m + 1) * P], p_sb[:, g % 2, m * P:(m + 1) * P], ident[:, :])
                last.then_inc(t_full[b], 1)

            def value(g):
                t, i = divmod(g, 16)
                fox, h, _, _ = head_of(i)
                first, n = keys_of(g)
                t_evacuated(pe, ("probs", g))
                if g == 0:
                    pe.wait_ge(va_ready, TILES)
                if g == HEADS:
                    pe.wait_ge(vb_ready, TILES)
                if t and h == 0:
                    pe.wait_ge(mix_ready, 2 * t - (1 if fox else 0))
                dst = o_ps[0 if fox else 1][:, h * HD:(h + 1) * HD]
                for m in range(n):
                    val = va[:, first + m, h * HD:(h + 1) * HD] if fox else \
                        vb[:, first + m, (h // GROUP) * HD:(h // GROUP + 1) * HD]
                    last = pe.matmul(dst, pT[:, g % 2, m * P:(m + 1) * P], val, start=(m == 0), stop=(m == n - 1))
                last.then_inc(value_done, 1)

            def mix(t):
                pe.wait_ge(mix_ready, 2 * t + 2)
                for half in range(2):
                    b = t_claim(("mix", t), half)
                    for m in range(4):
                        k = 4 * half + m
                        last = pe.transpose(t_ps[b][:, m * P:(m + 1) * P], o_sb[:, k * P:(k + 1) * P], ident[:, :])
                    last.then_inc(t_full[b], 1)

            def outp(n, t):
                if n == 0:
                    t_evacuated(pe, ("mix", t), 0)
                    t_evacuated(pe, ("mix", t), 1)
                    if t == 0:
                        pe.wait_ge(wout_loaded, 16)
                b = a_claim((f"out{n}", t))
                router = route(t - 1) if n == 0 and t else None
                for k in range(KT):
                    if router:
                        next(router)
                    last = pe.matmul(acc_ps[b][:, :], mixT[:, k, :], wout_sb[:, k, n * HALF:(n + 1) * HALF],
                                     start=(k == 0), stop=(k == KT - 1))
                last.then_inc(a_full[b], 1)
                if router:
                    next(router, None)

            def hn2_(t):
                pe.wait_ge(hn2_ready, t + 1)
                for half in range(2):
                    b = t_claim(("hn2", t), half)
                    for m in range(4):
                        k = 4 * half + m
                        last = pe.transpose(t_ps[b][:, m * P:(m + 1) * P], hn2[:, k * P:(k + 1) * P], ident[:, :])
                    last.then_inc(t_full[b], 1)

            def route(t):
                t_evacuated(pe, ("hn2", t), 0)
                t_evacuated(pe, ("hn2", t), 1)
                b = t_claim(("route", t))
                for k in range(KT):
                    last = pe.matmul(t_ps[b][:, 0:EXPERTS], hn2T[:, k, :], wr[:, k, :], start=(k == 0),
                                     stop=(k == KT - 1))
                    if k == KT - 1:
                        last.then_inc(t_full[b], 1)
                    yield

            def tokens():
                pe.wait_ge(onehot_ready, TILES)
                pe.wait_ge(late_consts, 3 + 2 * TILES)
                pe.wait_ge(h_ready, 2 * TILES)
                for j in range(TILES):
                    last = pe.matmul(gate_ps[0][:, 0:2], slot_oh[:, j, :], idx_rhs[:, j, 0:2], start=(j == 0),
                                     stop=(j == TILES - 1))
                last.then_inc(tok_psum, 1)

            def last_route(t):
                if t == TILES - 1:
                    for _ in route(t):
                        pass

            def place():
                pe.wait_ge(mask_ready, TILES)
                b = t_claim(("place",))
                for t in range(TILES):
                    dst = t_ps[b][:, t * EXPERTS:(t + 1) * EXPERTS]
                    for s in range(t):
                        pe.matmul(dst, ones_b[:, :], mask_b[:, s, :], start=(s == 0), stop=False)
                    pe.matmul(dst, before[:, :], mask_b[:, t, :], start=(t == 0), stop=True)
                for s in range(TILES):
                    last = pe.matmul(t_ps[b][0:EXPERTS, 128:129], mask_b[:, s, :], ones_b[:, 0:1], start=(s == 0),
                                     stop=(s == TILES - 1))
                last.then_inc(t_full[b], 1)

            does = {"hn": hn, "toep": toep, "proj": proj, "turn": turn, "decay": decay, "decay_turn": decay_turn,
                    "score": score, "probs": probs, "value": value, "mix": mix,
                    "out0": lambda t: outp(0, t), "out1": lambda t: outp(1, t), "hn2": hn2_, "route": last_route,
                    "place": place, "tokens": tokens}
            for s in order:
                if s[0] in does:
                    does[s[0]](*s[1:])

            def chunk(c):
                return ring[:, c * CHUNK_COLS:(c + 1) * CHUNK_COLS].rearrange("p (k n) -> p k n", k=2)

            def indices(s):
                pe.wait_ge(onehot_ready, s * TILES + TILES)
                pe.wait_ge(cols_copied, s * 2 + 2)
                for j in range(TILES):
                    last = pe.matmul(gate_ps[0][:, 0:5], slot_oh[:, j, :], idx_rhs[:, j, :], start=(j == 0),
                                     stop=(j == TILES - 1))
                last.then_inc(idx_psum, 1)

            def turn_rows(s):
                pe.wait_ge(gathered, s * 16 + 16)
                pe.wait_ge(idx_ready, s * 2 + 2)
                if later(s):
                    pe.wait_ge(gmin_ready, s)
                for k in range(KT):
                    last = pe.transpose(gate_ps[k // 4][:, (k % 4) * P:(k % 4 + 1) * P], gx[:, k * P:(k + 1) * P],
                                        ident[:, :])
                last.then_inc(x_transposed, 1)

            def product(dst, stat, c, k, n):
                kt = 2 * (c % 4) + k
                return pe.matmul(dst[n][:, :], stat[:, kt, :], chunk(c)[:, k, n * HALF:(n + 1) * HALF],
                                 start=(kt == 0), stop=False)

            def products(t, dst, stat, chunks):
                for c in chunks:
                    pe.wait_ge(w_loaded[c], t * 16 + 16)
                    for k in range(2):
                        for n in range(2):
                            last = product(dst, stat, c, k, n)
                    last.then_inc(chunk_used, 1)

            def bias(dst, col, n):
                return pe.matmul(dst[n][:, :], bias_sel[:, :], bias_tab[:, col + n * HALF:col + (n + 1) * HALF],
                                 start=False, stop=True)

            def turn_act(t, half):
                pe.wait_ge(act_ready, t * 2 + half + 1)
                if later(t):
                    pe.wait_ge(actT1_ready if half else actT0_ready, t)
                for m in range(4):
                    k = 4 * half + m
                    last = pe.transpose(turn_ps[half][:, m * P:(m + 1) * P], act_sb[:, k * P:(k + 1) * P], ident[:, :])
                last.then_inc(act_transposed, 1)

            def expert(t, ahead):
                pe.wait_ge(xT_ready, t * 2 + 2)
                products(t, gate_ps, xT, range(0, 2))
                if not later(t):
                    pe.wait_ge(over_step, 1)
                    pe.matmul(y_ps[0][0:EXPERTS, 0:1], before[0:EXPERTS, 0:EXPERTS], oext_b[:, :], start=True,
                              stop=True).then_inc(over_pe, 1)
                products(t, gate_ps, xT, range(2, 4))
                if not later(t):
                    pe.wait_ge(over_step, 2)
                    pe.matmul(y_ps[1][:, 0:48], ones_f[:, :], ooh[:, :, :].rearrange("p a j -> p (a j)"),
                              start=True, stop=True).then_inc(over_pe, 1)
                pe.wait_ge(sel_ready, t + 1)
                bias(gate_ps, 0, 0)
                bias(gate_ps, 0, 1).then_inc(gate_psum, 1)
                if later(t):
                    pe.wait_ge(up_ready, t * 2)
                products(t, up_ps, xT, range(4, 6))
                if ahead:
                    pe.wait_ge(gmin_ready, t + 1)
                    indices(t + 1)
                pe.wait_ge(w_loaded[6], t * 16 + 16)
                pe.wait_ge(w_loaded[7], t * 16 + 16)
                for n in range(2):
                    for c in (6, 7):
                        for k in range(2):
                            last = product(up_ps, xT, c, k, n)
                        if n == 1:
                            last.then_inc(chunk_used, 1)
                    bias(up_ps, D, n).then_inc(up_psum, 1)
                turn_act(t, 0)
                if ahead:
                    turn_rows(t + 1)
                if later(t):
                    pe.wait_ge(y_ready, t)
                else:
                    pe.wait_ge(over_ready, 1)
                pe.wait_ge(actT0_ready, t + 1)
                products(t, y_ps, actT, range(8, 9))
                turn_act(t, 1)
                products(t, y_ps, actT, range(9, 10))
                pe.wait_ge(actT1_ready, t + 1)
                products(t, y_ps, actT, range(10, 12))
                bias(y_ps, 2 * D, 0)
                bias(y_ps, 2 * D, 1).then_inc(y_psum, 1)

            pe.wait_ge(placed, 1)
            pe.wait_ge(cols_copied, 2)
            for j in range(TILES):
                last = pe.matmul(up_ps[0][:, 2:5], slot_oh[:, j, :], idx_rhs[:, j, 2:5], start=(j == 0),
                                 stop=(j == TILES - 1))
            last.then_inc(idx_psum, 1)
            turn_rows(0)
            pe.wait_ge(bias_split, 5)
            pe.wait_ge(idx_sum, 2)
            expert(0, True)
            with pe.Fori(1, EXPERTS - 1) as t:
                expert(t, True)
            expert(EXPERTS - 1, False)
            some = pe.value_load(over_tab[0:1, 32:33], min_val=0, max_val=1)
            with pe.If(some > 0):
                with pe.Fori(0, OVER) as j:
                    used = pe.value_load(over_tab[0:1, bass.ds(j + 32, 1)], min_val=0, max_val=1)
                    with pe.If(used > 0):
                        indices(j + EXPERTS)
                        turn_rows(j + EXPERTS)
                        expert(j + EXPERTS, False)


_INS = ["x", "norm_mix", "w_in", "b_forget", "q_norm_fox", "k_norm_fox", "q_norm_swa", "k_norm_swa", "sinks",
        "rel_bias", "w_out", "norm_moe", "w_router", "b_router", "w_up_gate", "b_up_gate", "w_down", "b_down"]


def kernel(**inputs):
    import numpy as _np
    import concourse.bacc as _bacc
    from concourse import mybir as _mybir
    from concourse.bass_utils import run_bass_kernel_spmd as _run

    nc = _bacc.Bacc("TRN2", target_bir_lowering=False, num_devices=1)
    arrays, args = {}, []
    for name in _INS:
        a = _np.ascontiguousarray(inputs[name])
        arrays[f"in_{name}_dram"] = a
        args.append(nc.dram_tensor(f"in_{name}_dram", a.shape, _mybir.dt.from_np(a.dtype), kind="ExternalInput").ap())
    table = bucket_table()
    arrays["in_buckets_dram"] = table
    args.append(nc.dram_tensor("in_buckets_dram", table.shape, _mybir.dt.float32, kind="ExternalInput").ap())
    args.append(nc.dram_tensor("out_0_dram", (OUT_ROWS, D), _mybir.dt.float32, kind="ExternalOutput").ap())
    layer_kernel(nc, *args)
    r = _run(nc, [arrays], core_ids=[0])
    return r.results[0]["out_0_dram"][:SEQ].reshape(1, SEQ, D)
```
